# Optimizing a Trainium2 kernel written in Bass

```python
import math
import jax, jax.numpy as jnp
from jax import lax
import numpy as np

D_MODEL = 1024
BATCH = 1
SEQ = 256
DEPTH = 2

CHUNK = 64
N_MIXERS = 2
N_A = (DEPTH + 1) // 2
N_B = DEPTH // 2
NORM_EPS = 1e-6

MLA_HEADS = 8
QK_NOPE = 128
QK_ROPE = 64
QK_HEAD = QK_NOPE + QK_ROPE
V_HEAD = 128
Q_LORA = 384
KV_LORA = 256
ROPE_BASE = 10000.0
Q_BLOCK = 128

LRU_WIDTH = D_MODEL
LRU_HEADS = 8
LRU_BLOCK = LRU_WIDTH // LRU_HEADS
CONV_WIDTH = 4
LRU_C = 8.0

DENSE_FF = 2816
N_EXPERTS = 8
TOP_K = 2
EXPERT_FF = 3584

MAX_POS_OFFSET = 8192

kernel_name = "hybrid_mla_rglru_moe_stream_encoder"

def rms_norm(x, g):
    x32 = x.astype(jnp.float32)
    y = x32 * lax.rsqrt(jnp.mean(x32 * x32, axis=-1, keepdims=True) + NORM_EPS)
    return (y * g.astype(jnp.float32)).astype(x.dtype)

def rope_tables(positions):
    inv = 1.0 / (ROPE_BASE ** (jnp.arange(0, QK_ROPE, 2, dtype=jnp.float32) / QK_ROPE))
    ang = positions.astype(jnp.float32)[..., None] * inv
    return jnp.cos(ang), jnp.sin(ang)

def apply_rope(x, cos, sin):
    x32 = x.astype(jnp.float32)
    half = QK_ROPE // 2
    x1, x2 = x32[..., :half], x32[..., half:]
    c = cos[:, :, None, :]
    s = sin[:, :, None, :]
    return jnp.concatenate([x1 * c - x2 * s, x1 * s + x2 * c], axis=-1).astype(x.dtype)

def chunk_causal_attention(q, k, v):
    b, s, h, dq = q.shape
    nb = s // Q_BLOCK
    scale = 1.0 / math.sqrt(dq)
    q_blocks = q.reshape(b, nb, Q_BLOCK, h, dq).transpose(1, 0, 2, 3, 4)
    key_chunk = jnp.arange(s) // CHUNK

    def one_block(args):
        qb, blk = args
        q_chunk = (blk * Q_BLOCK + jnp.arange(Q_BLOCK)) // CHUNK
        mask = key_chunk[None, :] <= q_chunk[:, None]
        sc = jnp.einsum('bqhd,bkhd->bhqk', qb, k, preferred_element_type=jnp.float32) * scale
        sc = jnp.where(mask[None, None], sc, -jnp.inf)
        p = jax.nn.softmax(sc, axis=-1)
        return jnp.einsum('bhqk,bkhd->bqhd', p.astype(v.dtype), v)

    out = lax.map(one_block, (q_blocks, jnp.arange(nb)))
    return out.transpose(1, 0, 2, 3, 4).reshape(b, s, h, v.shape[-1])

def mla_mixer(x, cos, sin, w_in, g_qa, w_qb, g_kva, w_kvb, g_qn, g_kn, w_o):
    b, s, _ = x.shape
    hcat = x @ w_in
    cq = hcat[..., :Q_LORA]
    ckv = hcat[..., Q_LORA:Q_LORA + KV_LORA]
    k_rope = hcat[..., Q_LORA + KV_LORA:]
    q = (rms_norm(cq, g_qa) @ w_qb).reshape(b, s, MLA_HEADS, QK_HEAD)
    kv = (rms_norm(ckv, g_kva) @ w_kvb).reshape(b, s, MLA_HEADS, QK_NOPE + V_HEAD)
    k_nope, v = kv[..., :QK_NOPE], kv[..., QK_NOPE:]
    k = jnp.concatenate(
        [k_nope, jnp.broadcast_to(k_rope[:, :, None, :], (b, s, MLA_HEADS, QK_ROPE))], axis=-1)
    q = rms_norm(q, g_qn)
    k = rms_norm(k, g_kn)
    q = jnp.concatenate([q[..., :QK_NOPE], apply_rope(q[..., QK_NOPE:], cos, sin)], axis=-1)
    k = jnp.concatenate([k[..., :QK_NOPE], apply_rope(k[..., QK_NOPE:], cos, sin)], axis=-1)
    o = chunk_causal_attention(q, k, v)
    return o.reshape(b, s, MLA_HEADS * V_HEAD) @ w_o

def rglru_mixer(x, w_in, b_in, conv_w, conv_b, w_gate_a, b_gate_a, w_gate_i, b_gate_i,
                lam, w_out, b_out):
    b, s, _ = x.shape
    hcat = x @ w_in + b_in
    gate_branch = jax.nn.gelu(hcat[..., :LRU_WIDTH], approximate=True)
    xb = hcat[..., LRU_WIDTH:]
    xp = jnp.pad(xb, ((0, 0), (CONV_WIDTH - 1, 0), (0, 0)))
    xc = conv_b + xp[:, 0:s] * conv_w[0]
    for j in range(1, CONV_WIDTH):
        xc = xc + xp[:, j:j + s] * conv_w[j]
    xh = xc.reshape(b, s, LRU_HEADS, LRU_BLOCK)
    r = jax.nn.sigmoid(jnp.einsum('bshi,hij->bshj', xh, w_gate_a) + b_gate_a).reshape(b, s, LRU_WIDTH)
    i = jax.nn.sigmoid(jnp.einsum('bshi,hij->bshj', xh, w_gate_i) + b_gate_i).reshape(b, s, LRU_WIDTH)
    log_a = LRU_C * r.astype(jnp.float32) * jax.nn.log_sigmoid(lam.astype(jnp.float32))
    a = jnp.exp(log_a)
    mult = jnp.sqrt(-jnp.expm1(2.0 * log_a))
    u = mult * (i * xc).astype(jnp.float32)

    def step(h_prev, inp):
        a_t, u_t = inp
        h_new = a_t * h_prev + u_t
        return h_new, h_new

    h0 = jnp.zeros((b, LRU_WIDTH), jnp.float32)
    _, hs = lax.scan(step, h0, (a.transpose(1, 0, 2), u.transpose(1, 0, 2)))
    y = hs.transpose(1, 0, 2).astype(x.dtype)
    return (y * gate_branch) @ w_out + b_out

def dense_swiglu(x, w1, w3, w2):
    return (jax.nn.silu(x @ w1) * (x @ w3)) @ w2

def moe_swiglu(x, w_router, b_router, w1, w3, w2):
    b, s, d = x.shape
    t = x.reshape(b * s, d)
    logits = jnp.dot(t, w_router, preferred_element_type=jnp.float32) + b_router.astype(jnp.float32)
    top_val, top_idx = lax.top_k(logits, TOP_K)
    top_w = jax.nn.softmax(top_val, axis=-1)
    gates = jnp.sum(jax.nn.one_hot(top_idx, N_EXPERTS, dtype=jnp.float32) * top_w[..., None], axis=1)
    out = jnp.zeros_like(t)
    for e in range(N_EXPERTS):
        he = jax.nn.silu(t @ w1[e]) * (t @ w3[e])
        out = out + gates[:, e:e + 1].astype(t.dtype) * (he @ w2[e])
    return out.reshape(b, s, d)

def _normal(k, shape, fan_in):
    return jax.random.normal(k, shape, jnp.float32) * (float(fan_in) ** -0.5)

def _gain(k, shape):
    return 1.0 + 0.02 * jax.random.normal(k, shape, jnp.float32)

def _bias(k, shape, scale=0.02):
    return scale * jax.random.normal(k, shape, jnp.float32)

def setup_inputs(seed: int = 0) -> dict:
    key = jax.random.key(seed)
    ks = jax.random.split(key, 40)
    d = D_MODEL
    x = jax.random.normal(ks[0], (BATCH, SEQ, d), jnp.float32)
    offset = jax.random.randint(ks[1], (BATCH, 1), 0, MAX_POS_OFFSET)
    positions = (jnp.arange(SEQ, dtype=jnp.int32)[None, :] + offset).astype(jnp.int32)

    norm_mix = _gain(ks[2], (DEPTH, d))
    norm_ffn = _gain(ks[3], (DEPTH, d))

    mla_w_in = _normal(ks[4], (N_A, d, Q_LORA + KV_LORA + QK_ROPE), d)
    mla_g_qa = _gain(ks[5], (N_A, Q_LORA))
    mla_w_qb = _normal(ks[6], (N_A, Q_LORA, MLA_HEADS * QK_HEAD), Q_LORA)
    mla_g_kva = _gain(ks[7], (N_A, KV_LORA))
    mla_w_kvb = _normal(ks[8], (N_A, KV_LORA, MLA_HEADS * (QK_NOPE + V_HEAD)), KV_LORA)
    mla_g_qn = _gain(ks[9], (N_A, QK_HEAD))
    mla_g_kn = _gain(ks[10], (N_A, QK_HEAD))
    mla_w_o = _normal(ks[11], (N_A, MLA_HEADS * V_HEAD, d), MLA_HEADS * V_HEAD)

    lru_w_in = _normal(ks[12], (N_B, d, 2 * LRU_WIDTH), d)
    lru_b_in = _bias(ks[13], (N_B, 2 * LRU_WIDTH))
    lru_conv_w = _normal(ks[14], (N_B, CONV_WIDTH, LRU_WIDTH), CONV_WIDTH)
    lru_conv_b = _bias(ks[15], (N_B, LRU_WIDTH))
    lru_w_gate_a = _normal(ks[16], (N_B, LRU_HEADS, LRU_BLOCK, LRU_BLOCK), LRU_BLOCK)
    lru_b_gate_a = _bias(ks[17], (N_B, LRU_HEADS, LRU_BLOCK))
    lru_w_gate_i = _normal(ks[18], (N_B, LRU_HEADS, LRU_BLOCK, LRU_BLOCK), LRU_BLOCK)
    lru_b_gate_i = _bias(ks[19], (N_B, LRU_HEADS, LRU_BLOCK))
    u = jax.random.uniform(ks[20], (N_B, LRU_WIDTH), jnp.float32, minval=0.9, maxval=0.999)
    sig = u ** (1.0 / LRU_C)
    lru_lambda = jnp.log(sig) - jnp.log1p(-sig)
    lru_w_out = _normal(ks[21], (N_B, LRU_WIDTH, d), LRU_WIDTH)
    lru_b_out = _bias(ks[22], (N_B, d))

    ffn_w1 = _normal(ks[23], (N_A, d, DENSE_FF), d)
    ffn_w3 = _normal(ks[24], (N_A, d, DENSE_FF), d)
    ffn_w2 = _normal(ks[25], (N_A, DENSE_FF, d), DENSE_FF)

    moe_w_router = _normal(ks[26], (N_B, d, N_EXPERTS), d)
    moe_b_router = _bias(ks[27], (N_B, N_EXPERTS), 0.01)
    moe_w1 = _normal(ks[28], (N_B, N_EXPERTS, d, EXPERT_FF), d)
    moe_w3 = _normal(ks[29], (N_B, N_EXPERTS, d, EXPERT_FF), d)
    moe_w2 = _normal(ks[30], (N_B, N_EXPERTS, EXPERT_FF, d), EXPERT_FF)

    return {
        "x": x, "positions": positions, "norm_mix": norm_mix, "norm_ffn": norm_ffn,
        "mla_w_in": mla_w_in, "mla_g_qa": mla_g_qa, "mla_w_qb": mla_w_qb,
        "mla_g_kva": mla_g_kva, "mla_w_kvb": mla_w_kvb, "mla_g_qn": mla_g_qn,
        "mla_g_kn": mla_g_kn, "mla_w_o": mla_w_o,
        "lru_w_in": lru_w_in, "lru_b_in": lru_b_in, "lru_conv_w": lru_conv_w,
        "lru_conv_b": lru_conv_b, "lru_w_gate_a": lru_w_gate_a, "lru_b_gate_a": lru_b_gate_a,
        "lru_w_gate_i": lru_w_gate_i, "lru_b_gate_i": lru_b_gate_i, "lru_lambda": lru_lambda,
        "lru_w_out": lru_w_out, "lru_b_out": lru_b_out,
        "ffn_w1": ffn_w1, "ffn_w3": ffn_w3, "ffn_w2": ffn_w2,
        "moe_w_router": moe_w_router, "moe_b_router": moe_b_router,
        "moe_w1": moe_w1, "moe_w3": moe_w3, "moe_w2": moe_w2,
    }

def reference(x, positions, norm_mix, norm_ffn,
              mla_w_in, mla_g_qa, mla_w_qb, mla_g_kva, mla_w_kvb, mla_g_qn, mla_g_kn, mla_w_o,
              lru_w_in, lru_b_in, lru_conv_w, lru_conv_b, lru_w_gate_a, lru_b_gate_a,
              lru_w_gate_i, lru_b_gate_i, lru_lambda, lru_w_out, lru_b_out,
              ffn_w1, ffn_w3, ffn_w2,
              moe_w_router, moe_b_router, moe_w1, moe_w3, moe_w2):
    cos, sin = rope_tables(positions)
    for i in range(DEPTH):
        j = i // N_MIXERS
        xn = rms_norm(x, norm_mix[i])
        if i % N_MIXERS == 0:
            x = x + mla_mixer(xn, cos, sin, mla_w_in[j], mla_g_qa[j], mla_w_qb[j], mla_g_kva[j],
                              mla_w_kvb[j], mla_g_qn[j], mla_g_kn[j], mla_w_o[j])
        else:
            x = x + rglru_mixer(xn, lru_w_in[j], lru_b_in[j], lru_conv_w[j], lru_conv_b[j],
                                lru_w_gate_a[j], lru_b_gate_a[j], lru_w_gate_i[j], lru_b_gate_i[j],
                                lru_lambda[j], lru_w_out[j], lru_b_out[j])
        xn = rms_norm(x, norm_ffn[i])
        if i % 2 == 0:
            x = x + dense_swiglu(xn, ffn_w1[j], ffn_w3[j], ffn_w2[j])
        else:
            x = x + moe_swiglu(xn, moe_w_router[j], moe_b_router[j], moe_w1[j], moe_w3[j], moe_w2[j])
    return x


_drawn_inputs = setup_inputs


def setup_inputs(seed=0):
    import zlib

    import numpy as np

    out = dict(_drawn_inputs(seed))
    spreads = {}
    factors = {'mla_g_qa': 4.572,
     'mla_g_qn': 3.667,
     'mla_g_kn': 4.612,
     'lru_b_gate_a': 31.0,
     'lru_b_gate_i': 19.208,
     'moe_b_router': 8.0}
    for name, (base, spread) in spreads.items():
        noise = np.random.default_rng([zlib.crc32(name.encode()), seed]).standard_normal(out[name].shape)
        drawn = base * np.exp(spread * noise) if base else spread * noise
        out[name] = __import__('jax').numpy.asarray(drawn.astype(out[name].dtype))
    for name, factor in factors.items():
        out[name] = (out[name] * factor).astype(out[name].dtype)
    return out
```

```python
from contextlib import ExitStack

import numpy as np

import concourse.bass as bass
from concourse import mybir

ALU = mybir.AluOpType
ACT = mybir.ActivationFunctionType
AX = mybir.AxisListType
F32 = mybir.dt.float32
F32R = mybir.dt.float32r
I32 = mybir.dt.int32
U32 = mybir.dt.uint32

P = 128
BANK = 512
SBUF_BASE, SBUF_END = 16512, 229344
NORM_EPS = 1e-6
ROPE_BASE = 10000.0
UNIT = 2048
RAW_SLOTS = 14
ATT_SLOTS = 5
SPLIT_SLOTS = 3
NEG = -1.0e30
MISS = 1000.0
TWO_PI_A = 6.28125
TWO_PI_B = round((2 * np.pi - TWO_PI_A) * 2 ** 21) / 2 ** 21
TWO_PI_C = float(2 * np.pi - TWO_PI_A - TWO_PI_B)
ROUND_MAGIC = 12582912.0
PI_FLOOR = 3.1415925


class Region:

    def __init__(self, nc, base, size):
        self.nc, self.base, self.at, self.end = nc, base, base, base + size

    def take(self, name, shape, dtype=F32):
        size = 4 * int(np.prod(shape[1:]))
        tensor = self.nc.alloc_sbuf_tensor_at(name, shape, dtype, offset=self.at)
        self.at += (size + 31) // 32 * 32
        assert self.at <= self.end, (name, self.at, self.end)
        return tensor

    def skip(self, size):
        part = Region(self.nc, self.at, size)
        self.at += size
        assert self.at <= self.end
        return part


class Chain:

    def __init__(self, engine, sem):
        self.engine, self.sem, self.count = engine, sem, 0

    def step(self, instruction):
        instruction.then_inc(self.sem, 1)
        self.count += 1

    def settle(self):
        self.engine.wait_ge(self.sem, self.count)

    def link(self, instruction):
        self.step(instruction)
        self.settle()


def encoder_trunk(nc, x, positions, norm_mix, norm_ffn, mla_w_in, mla_g_qa, mla_w_qb, mla_g_kva,
                  mla_w_kvb, mla_g_qn, mla_g_kn, mla_w_o, lru_w_in, lru_b_in, lru_conv_w,
                  lru_conv_b, lru_w_gate_a, lru_b_gate_a, lru_w_gate_i, lru_b_gate_i, lru_lambda,
                  lru_w_out, lru_b_out, ffn_w1, ffn_w3, ffn_w2, moe_w_router, moe_b_router,
                  moe_w1, moe_w3, moe_w2, inv_freq, out):
    _, SEQ, D = x.shape
    TT = SEQ // P
    KD = D // P
    Q_LORA, KV_LORA = mla_g_qa.shape[1], mla_g_kva.shape[1]
    QK_HEAD = mla_g_qn.shape[1]
    HEADS = mla_w_qb.shape[2] // QK_HEAD
    V_HEAD = mla_w_o.shape[1] // HEADS
    NOPE = mla_w_kvb.shape[2] // HEADS - V_HEAD
    ROPE = QK_HEAD - NOPE
    HALF = ROPE // 2
    CAT = mla_w_in.shape[2]
    LAT = (Q_LORA + KV_LORA) // P
    KQ, KKV = Q_LORA // P, KV_LORA // P
    FF = ffn_w1.shape[2]
    LRU_HEADS, E = lru_w_gate_a.shape[1], moe_w1.shape[1]
    EFF = moe_w1.shape[3]
    assert (TT, KD, HEADS, NOPE, ROPE, V_HEAD, E, LRU_HEADS) == (2, 8, 8, 128, 64, 128, 8, 8)

    def rows_of(w, c0, n, cols=slice(None)):
        return w[c0 * P:(c0 + n) * P, cols].rearrange("(k p) n -> p k n", p=P)

    units = []

    def add(*parts):
        units.append(parts)
        return len(units) - 1

    w_in, w_qb, w_kvb, w_o = mla_w_in[0], mla_w_qb[0], mla_w_kvb[0], mla_w_o[0]
    U_WIN = [add((0, rows_of(w_in, 2 * i, 2))) for i in range(KD // 2)]
    U_KV = [add((0, rows_of(w_kvb, 0, KKV, slice(i * 1024, (i + 1) * 1024)))) for i in range(2)]
    U_Q = [add((0, rows_of(w_qb, 0, KQ, slice(i * BANK, (i + 1) * BANK)))) for i in range(3)]
    U_WO = [add((0, rows_of(w_o, 2 * i, 2))) for i in range(4)]
    N_ATT = len(units)
    FSTEPS = FF // 256
    assert FF == 256 * FSTEPS
    U_F1, U_F3, U_F2 = {}, {}, {}
    for s in range(FSTEPS + 1):
        cols = slice(s * 256, (s + 1) * 256)
        if s < FSTEPS:
            U_F1[s] = add((0, rows_of(ffn_w1[0], 0, KD, cols)))
        if s:
            U_F2[s - 1] = add((0, rows_of(ffn_w2[0], 2 * (s - 1), 2)))
        if s < FSTEPS:
            U_F3[s] = add((0, rows_of(ffn_w3[0], 0, KD, cols)))
    LSTEPS = LRU_HEADS // 2
    U_X, U_G, U_GA, U_O = {}, {}, {}, {}
    for s in range(LSTEPS + 1):
        if s < LSTEPS:
            U_X[s] = add((0, rows_of(lru_w_in[0], 0, KD, slice(D + s * 256, D + (s + 1) * 256))))
            U_G[s] = add((0, rows_of(lru_w_in[0], 0, KD, slice(s * 256, (s + 1) * 256))))
        if s:
            U_O[s - 1] = add((0, rows_of(lru_w_out[0], 2 * (s - 1), 2)))
        if s < LSTEPS:
            U_GA[s] = add((0, lru_w_gate_a[0, 2 * s:2 * s + 2].rearrange("h i j -> i h j")),
                          (256, lru_w_gate_i[0, 2 * s:2 * s + 2].rearrange("h i j -> i h j")))
    N_PRE = len(units)
    width = [max(c + p.shape[1] * p.shape[2] for c, p in u) for u in units]

    MSTEPS = EFF // BANK
    assert EFF == MSTEPS * BANK
    M_W1, M_W3, M_W2 = {}, {}, {}
    body_units = []
    for t in range(MSTEPS + 1):
        if t < MSTEPS:
            for name, table in (("w1", M_W1), ("w3", M_W3)):
                for half in range(2):
                    table[t, half] = len(body_units)
                    body_units.append((name, t, half))
        if t:
            for half in range(2):
                M_W2[t - 1, half] = len(body_units)
                body_units.append(("w2", t - 1, half))
    N_BODY = len(body_units)
    assert N_BODY % RAW_SLOTS == 0 and N_BODY % SPLIT_SLOTS == 0
    OCC = N_BODY // RAW_SLOTS

    order = [(N_ATT + i) % ATT_SLOTS for i in range(ATT_SLOTS)] + list(range(ATT_SLOTS, RAW_SLOTS))

    def slot_of(g):
        return g % ATT_SLOTS if g < N_ATT else order[(g - N_ATT) % RAW_SLOTS]

    landed_at, count = [], [0] * RAW_SLOTS
    for g, parts in enumerate(units):
        count[slot_of(g)] += 16 * len(parts)
        landed_at.append(count[slot_of(g)])
    slot_count = list(count)

    sbuf = Region(nc, SBUF_BASE, SBUF_END - SBUF_BASE)
    res = sbuf.take("residual", [P, TT, D])
    act_hi = sbuf.take("act_hi", [P, KD * SEQ], F32R)
    act_lo = sbuf.take("act_lo", [P, KD * SEQ], F32R)
    mid = sbuf.skip(18432)
    raw_region = sbuf.skip(RAW_SLOTS * UNIT * 4)
    w_hi = [sbuf.take(f"w_hi{i}", [P, UNIT], F32R) for i in range(SPLIT_SLOTS)]
    w_lo = [sbuf.take(f"w_lo{i}", [P, UNIT], F32R) for i in range(SPLIT_SLOTS)]
    raw = [Region(nc, raw_region.base + i * UNIT * 4, UNIT * 4).take(f"w_raw{i}", [P, UNIT])
           for i in range(RAW_SLOTS)]
    ident = sbuf.take("ident", [P, P])
    rows = sbuf.take("vector_rows", [P, P])
    lam = [sbuf.take(f"lam{i}", [P, LRU_HEADS]) for i in range(6)]
    cols = sbuf.take("vector_cols", [P, P])
    ones = sbuf.take("ones", [P, P])
    before = sbuf.take("before", [P, P])
    slot_ids = sbuf.take("slot_ids", [P, 2 * P])
    expert_ids = sbuf.take("expert_ids", [P, E])
    w_router = sbuf.take("w_router", [P, KD, E])
    b_router = sbuf.take("b_router", [P, E])
    sumsq = sbuf.take("sumsq", [P, 8])
    rstd = sbuf.take("rstd", [P, 8])
    minus_half = sbuf.take("minus_half", [P, 16])
    rank = sbuf.take("rank", [P, TT, E])
    gates = sbuf.take("gates", [P, TT, E])
    counts = sbuf.take("counts", [P, E], I32)
    slot_gate = sbuf.take("slot_gate", [P, 1])
    decay = sbuf.take("decay", [P, 2, LRU_HEADS])
    bias_n = sbuf.take("bias_neg", [P, 2, LRU_HEADS])

    def over(base, size):
        return Region(nc, base, size)

    m = over(mid.base, 18432)
    trig = [m.take(f"trig{i}", [P, TT, HALF]) for i in range(4)]
    m = over(mid.base + 8192, 18432 - 8192)
    xn = m.take("x_normed", [P, TT, D])
    m = over(mid.base, 18432)
    kr = m.take("k_rope", [P, TT, HEADS, ROPE])
    qr = m.take("q_rope", [P, TT, HEADS, ROPE])
    rope_t = [m.take(f"rope_t{i}", [P, TT, HEADS, HALF]) for i in range(4)]
    junk = over(mid.base + 8192, 8192).take("squares", [P, UNIT])
    m = over(mid.base, 18432)
    f_h = [m.take(f"ffn_h{i}", [P, BANK]) for i in range(2)]
    f_hi = m.take("ffn_h_hi", [P, BANK], F32R)
    f_lo = m.take("ffn_h_lo", [P, BANK], F32R)
    m = over(mid.base, 18432)
    xpad = m.take("xb_padded", [P, 2, SEQ + 4])
    xc = m.take("xb_conv", [P, 2, SEQ])
    lc_hi = m.take("lru_hi", [P, 2, SEQ], F32R)
    lc_lo = m.take("lru_lo", [P, 2, SEQ], F32R)
    gate = m.take("gate", [P, 2, SEQ])
    ra = m.take("r_then_a", [P, 2, SEQ])
    iu = m.take("i_then_u", [P, 2, SEQ])
    tm = m.take("t_then_mult", [P, 2, SEQ])
    gx = m.take("gate_x", [P, 1, SEQ])
    m = over(mid.base, 18432)
    rx = m.take("router_x", [P, TT, D])
    rxT = m.take("router_xT", [P, KD, SEQ])
    rsm = [m.take(f"router_small{i}", [P, TT, 8]) for i in range(10)]
    ridx = m.take("router_idx", [P, TT, 8], U32)
    m = over(mid.base, 18432)
    in_hi = m.take("expert_in_hi", [P, D], F32R)
    in_lo = m.take("expert_in_lo", [P, D], F32R)
    y_at = m.at
    e_h = [m.take(f"expert_h{i}", [P, BANK]) for i in range(2)]
    hT_hi = m.take("expert_hT_hi", [P, BANK], F32R)
    hT_lo = m.take("expert_hT_lo", [P, BANK], F32R)
    y_m = over(y_at, 8192)
    y_hi = y_m.take("expert_out_hi", [P, D], F32R)
    y_lo = y_m.take("expert_out_lo", [P, D], F32R)
    sel = m.take("select", [P, TT, P], F32R)
    selT = m.take("select_T", [P, SEQ], F32R)

    far = over(raw_region.base + ATT_SLOTS * UNIT * 4, (RAW_SLOTS - ATT_SLOTS) * UNIT * 4)
    hcat_at = far.at
    hcat = far.take("hcat", [P, TT, CAT])
    lat_at = far.at
    lat_hi = far.take("latent_hi", [P, LAT, SEQ], F32R)
    lat_lo = far.take("latent_lo", [P, LAT, SEQ], F32R)
    qn = far.take("q", [P, TT, HEADS, QK_HEAD])
    kn = far.take("k_nope", [P, TT, HEADS, NOPE])
    vt = far.take("v", [P, TT, HEADS, V_HEAD])
    qT = far.take("qT_nope", [P, HEADS, SEQ])
    qrT = far.take("qT_rope", [P, HEADS, SEQ])
    kT = far.take("kT_nope", [P, HEADS, SEQ])
    mask = far.take("mask", [P, 3 * P])
    g_rope = far.take("g_rope", [P, 2 * ROPE])
    pos_i = far.take("pos_i", [P, TT], I32)
    freq = far.take("freq", [P, HALF])
    cos = far.take("cos", [P, TT, HALF])
    sin = far.take("sin", [P, TT, HALF])
    ssh = far.take("head_sumsq", [P, 2, TT * HEADS])
    rsh = far.take("head_rstd", [P, 2, TT * HEADS])
    ssr = far.take("rope_sumsq", [P, TT])
    krT = over(hcat_at, 5632).take("kT_rope", [P, HEADS // 2, SEQ])
    soft = over(lat_at, 10240)
    sc = [soft.take(f"scores{i}", [P, 3 * P]) for i in range(2)]
    pr = [soft.take(f"probs{i}", [P, 3 * P]) for i in range(2)]
    prT = [soft.take(f"probs_T{i}", [P, 3 * P]) for i in range(2)]
    smax = soft.take("smax", [P, HEADS, 2])
    ssum = soft.take("ssum", [P, HEADS, 2])
    sinv = soft.take("sinv", [P, HEADS, 2])

    R_MIX, R_FFN, R_QA, R_KVA, R_QN, R_KN, R_BIN, R_CW, R_CB, R_BA, R_BI, R_LAM, R_BO, R_GR = (
        0, 16, 32, 35, 37, 38, 39, 55, 87, 95, 103, 111, 119, 127)
    vectors = [
        (R_MIX, norm_mix.rearrange("l (k p) -> (l k) p", p=P)),
        (R_FFN, norm_ffn.rearrange("l (k p) -> (l k) p", p=P)),
        (R_QA, mla_g_qa.rearrange("l (k p) -> (l k) p", p=P)),
        (R_KVA, mla_g_kva.rearrange("l (k p) -> (l k) p", p=P)),
        (R_QN, mla_g_qn[:, 0:NOPE]), (R_KN, mla_g_kn[:, 0:NOPE]),
        (R_BIN, lru_b_in.rearrange("l (k p) -> (l k) p", p=P)),
        (R_CW, lru_conv_w[0].rearrange("j (k p) -> (j k) p", p=P)),
        (R_CB, lru_conv_b.rearrange("l (k p) -> (l k) p", p=P)),
        (R_BA, lru_b_gate_a[0]), (R_BI, lru_b_gate_i[0]),
        (R_LAM, lru_lambda.rearrange("l (k p) -> (l k) p", p=P)),
        (R_BO, lru_b_out.rearrange("l (k p) -> (l k) p", p=P)),
    ]

    ctx = ExitStack()
    with ctx:
        ps = ctx.enter_context(nc.psum_tensor("ps", [P, 8, BANK], F32))

        def sem(name):
            return ctx.enter_context(nc.semaphore(name))

        raw_landed = [sem(f"raw_landed{i}") for i in range(RAW_SLOTS)]
        hi_ready = sem("hi_ready")
        lo_ready = sem("lo_ready")
        unit_used = sem("unit_used")
        trig_ready = sem("trig_ready")
        x_landed, vec_landed, small_landed, pos_landed = (
            sem("x_landed"), sem("vec_landed"), sem("small_landed"), sem("pos_landed"))
        const_ready = sem("const_ready")
        rows_turned = sem("rows_turned")
        cols_ready = sem("cols_ready")
        sq_act, sq_dve = sem("sq_act"), sem("sq_dve")
        rstd_ready = sem("rstd_ready")
        xn_ready, xn_turned = sem("xn_ready"), sem("xn_turned")
        act_hi_ready, act_lo_ready = sem("act_hi_ready"), sem("act_lo_ready")
        res_ready = sem("res_ready")
        cat_ready = sem("cat_ready")
        cat_sq = sem("cat_sq")
        lat_rstd, lat_scaled, lat_turned = sem("lat_rstd"), sem("lat_scaled"), sem("lat_turned")
        lat_hi_ready, lat_lo_ready = sem("lat_hi_ready"), sem("lat_lo_ready")
        kv0_copied, kv1_copied, q_copied = sem("kv0_copied"), sem("kv1_copied"), sem("q_copied")
        head_sq, head_rstd = sem("head_sq"), sem("head_rstd")
        kq_normed, kq_turned = sem("kq_normed"), sem("kq_turned")
        kqT_act, kqT_dve = sem("kqT_act"), sem("kqT_dve")
        qrT_zeroed = sem("qrT_zeroed")
        scores_ready, smax_ready, exp_ready = sem("scores_ready"), sem("smax_ready"), sem("exp_ready")
        probs_ready, probs_turned, probsT_ready = (
            sem("probs_ready"), sem("probs_turned"), sem("probsT_ready"))
        pv_ready, o_hi_ready, o_lo_ready = sem("pv_ready"), sem("o_hi_ready"), sem("o_lo_ready")
        f_silu, f_h_ready, f_hi_ready, f_lo_ready = (
            sem("f_silu"), sem("f_h_ready"), sem("f_hi_ready"), sem("f_lo_ready"))
        xb_ready, conv_ready, xc_hi_ready, xc_lo_ready = (
            sem("xb_ready"), sem("conv_ready"), sem("xc_hi_ready"), sem("xc_lo_ready"))
        gx_ready, gin_ready, gexp_ready, gate_ready = (
            sem("gx_ready"), sem("gin_ready"), sem("gexp_ready"), sem("gate_ready"))
        sig_exp, sig_ready, at_ready, v_ready, mult_ready = (
            sem("sig_exp"), sem("sig_ready"), sem("at_ready"), sem("v_ready"), sem("mult_ready"))
        y_ready, y_hi_ready, y_lo_ready = sem("y_ready"), sem("y_hi_ready"), sem("y_lo_ready")
        lam_exp, lam_ready = sem("lam_exp"), sem("lam_ready")
        gain_rows, rx_ready, rx_turned, rxT_ready = (
            sem("gain_rows"), sem("rx_ready"), sem("rx_turned"), sem("rxT_ready"))
        tok_hi_ready, tok_lo_ready = sem("tok_hi_ready"), sem("tok_lo_ready")
        logits_ready, top_ready, top_exp, mask_ready, ranks_ready, routed = (
            sem("logits_ready"), sem("top_ready"), sem("top_exp"), sem("mask_ready"),
            sem("ranks_ready"), sem("routed"))
        sel_ready, gathered, selT_turned = sem("sel_ready"), sem("gathered"), sem("selT_turned")
        in_hi_ready, in_lo_ready = sem("in_hi_ready"), sem("in_lo_ready")
        y_lo_split, y_zeroed = sem("y_lo_split"), sem("y_zeroed")
        selT_ready, gate_col_ready = sem("selT_ready"), sem("gate_col_ready")
        silu_ready, h_ready = sem("silu_ready"), sem("h_ready")
        h_turned, hT_hi_ready, hT_lo_ready = sem("h_turned"), sem("hT_hi_ready"), sem("hT_lo_ready")
        out_hi_ready = sem("out_hi_ready")
        scattered = sem("scattered")
        act_own, dve_own, pool_own, out_sem = (
            sem("act_own"), sem("dve_own"), sem("pool_own"), sem("out_sem"))

        R_PRE = 3 * 2 * TT

        block = ctx.enter_context(nc.Block())

        def experts(engine, body, prologue=None, last=None, extra=None):
            if prologue:
                prologue()
            with engine.Fori(0, E - 1 if last else E) as e:
                body(e, e, 0)
            if last:
                last(E - 1, E - 1, 0)
            engine.wait_ge(routed, 1)
            done = engine.alloc_register(f"passes_{engine.engine.name}")
            engine.reg_mov(done, E)
            with engine.Fori(0, E) as e:
                n_tokens = engine.value_load(counts[0:1, bass.ds(e, 1)], min_val=0, max_val=SEQ)
                with engine.If(n_tokens > P):
                    (extra or body)(engine.snap(done, min_val=E, max_val=2 * E), e, P)
                    engine.reg_add(done, done, 1)
            return engine.snap(done, min_val=E, max_val=2 * E)

        def held(engine, value):
            return value if isinstance(value, int) else engine.snap(value)

        def lru_order(split, x_work, g_work, a_work, conv_split):
            for g in range(U_X[0] - 1, N_PRE):
                if g + SPLIT_SLOTS < N_PRE:
                    split(g + SPLIT_SLOTS)
                for s in range(LSTEPS):
                    if g == U_X[s]:
                        x_work(s)
                    elif g == U_G[s]:
                        g_work(s)
                    elif g == U_GA[s]:
                        a_work(s)
                    elif g == U_O[s] and s + 1 < LSTEPS:
                        conv_split(s + 1)

        @block.sync
        def _(sp):
            for i in range(TT):
                sp.dma_start(res[:, i, :], x[0, i * P:(i + 1) * P, :]).then_inc(x_landed, 16)
            for g, parts in enumerate(units):
                if g < N_ATT:
                    if g >= ATT_SLOTS:
                        sp.wait_ge(lo_ready, g - ATT_SLOTS + 1)
                elif g < N_ATT + ATT_SLOTS:
                    sp.wait_ge(lo_ready, g - ATT_SLOTS + 1)
                elif g < N_ATT + RAW_SLOTS:
                    sp.wait_ge(pv_ready, HEADS)
                else:
                    sp.wait_ge(lo_ready, g - RAW_SLOTS + 1)
                for c0, src in parts:
                    n, w = src.shape[1], src.shape[2]
                    dst = raw[slot_of(g)][:, c0:c0 + n * w].rearrange("p (k n) -> p k n", k=n)
                    sp.dma_start(dst, src).then_inc(raw_landed[slot_of(g)], 16)

            def body(n, e, off):
                base = sp.snap(n * N_BODY)
                w1, w3, w2 = (w[0, bass.ds(e, 1)] for w in (moe_w1, moe_w3, moe_w2))
                for u, (name, t, half) in enumerate(body_units):
                    if name == "w2":
                        r0 = t * BANK + half * 256
                        src = w2[:, r0:r0 + 256, :].rearrange("o (k p) n -> p (o k) n", p=P)
                    else:
                        w = w1 if name == "w1" else w3
                        src = w[:, half * 512:half * 512 + 512, t * BANK:(t + 1) * BANK]
                        src = src.rearrange("o (k p) n -> p (o k) n", p=P)
                    slot = slot_of(N_PRE + u)
                    dst = raw[slot][:, :].rearrange("p (k n) -> p k n", k=src.shape[1])
                    sp.wait_ge(lo_ready, base + (N_PRE + u - RAW_SLOTS + 1))
                    sp.dma_start(dst, src).then_inc(raw_landed[slot], 16)

            done = experts(sp, body)
            sp.wait_ge(res_ready, sp.snap(done * 4 + (R_PRE + 4)))
            for i in range(TT):
                sp.dma_start(out[0, i * P:(i + 1) * P, :], res[:, i, :]).then_inc(out_sem, 16)
            sp.wait_ge(out_sem, 16 * TT)

        @block.gpsimd
        def _(pool):
            own = Chain(pool, pool_own)
            own.step(pool.memset(ident[:], 0.0))
            own.step(pool.memset(before[:], 1.0))
            own.step(pool.memset(mask[:], 0.0))
            own.settle()
            pool.affine_select(out=ident[:], in_=ident[:], compare_op=ALU.not_equal, fill=1.0,
                               base=0, pattern=[[-1, P]], channel_multiplier=1).then_inc(const_ready, 1)
            own.step(pool.memset(minus_half[:], -0.5))
            own.step(pool.memset(ones[:], 1.0))
            own.step(pool.affine_select(out=before[:], in_=before[:], compare_op=ALU.is_gt, fill=0.0,
                                        base=0, pattern=[[1, P]], channel_multiplier=-1))
            for c0 in (P // 2, 3 * P - P // 2):
                own.step(pool.memset(mask[0:P // 2, c0:c0 + P // 2], NEG))
            own.step(pool.iota(slot_ids[:], pattern=[[1, 2 * P]], base=0, channel_multiplier=0,
                               allow_small_or_imprecise_dtypes=True))
            own.step(pool.iota(expert_ids[:], pattern=[[1, E]], base=0, channel_multiplier=0,
                               allow_small_or_imprecise_dtypes=True))
            own.step(pool.memset(qrT[:], 0.0))
            own.settle()
            pool.memset(sumsq[:, 7:8], 0.0).then_inc(const_ready, 1)

            def power(dst, src, n, scale, bias, done):
                own.link(pool.tensor_scalar(dst, src, scale, bias, ALU.mult, ALU.add))
                pool.tensor_tensor(dst, dst, minus_half[:, 0:n], ALU.pow).then_inc(done, 1)

            def norm(i):
                pool.wait_ge(sq_act, i + 1)
                pool.wait_ge(sq_dve, i + 1)
                power(rstd[:, 0:2], sumsq[:, 0:2], 2, 1.0 / D, NORM_EPS, rstd_ready)

            norm(0)
            pool.wait_ge(cat_sq, 4)
            own.link(pool.tensor_scalar(rstd[:, 2:4], sumsq[:, 2:4], 1.0 / Q_LORA, NORM_EPS, ALU.mult, ALU.add))
            own.link(pool.tensor_scalar(rstd[:, 4:6], sumsq[:, 4:6], 1.0 / KV_LORA, NORM_EPS, ALU.mult, ALU.add))
            pool.tensor_tensor(rstd[:, 2:6], rstd[:, 2:6], minus_half[:, 0:4], ALU.pow).then_inc(lat_rstd, 1)
            pool.wait_ge(head_sq, 16)
            power(rsh[:, 0, :], ssh[:, 0, :], 16, 1.0 / QK_HEAD, NORM_EPS, head_rstd)
            pool.wait_ge(head_sq, 32)
            power(rsh[:, 1, :], ssh[:, 1, :], 16, 1.0, QK_HEAD * NORM_EPS, head_rstd)
            for i in range(1, 4):
                norm(i)
            pool.wait_ge(routed, 1)
            pool.memset(y_hi[:].bitcast(F32), 0.0).then_inc(y_zeroed, 1)

        def split_ap(g):
            return w_hi[g % SPLIT_SLOTS], w_lo[g % SPLIT_SLOTS]

        @block.tensor
        def _(pe):
            def product(dst, a, b, start, stop):
                pe.matmul(dst, a[0], b[0], start=start, stop=False)
                pe.matmul(dst, a[0], b[1], start=False, stop=False)
                return pe.matmul(dst, a[1], b[0], start=False, stop=stop)

            def parts(pair, *index):
                return tuple(t[index] for t in pair)

            acts = (act_hi, act_lo)

            def token_block(k, i):
                return tuple(t[:, k * SEQ + i * P:k * SEQ + (i + 1) * P] for t in acts)

            def tokens(k):
                return tuple(t[:, k * SEQ:(k + 1) * SEQ] for t in acts)

            def cols_of(g, c0, n):
                return tuple(t[:, c0:c0 + n] for t in split_ap(g))

            def use(g):
                pe.wait_ge(lo_ready, g + 1)

            pe.wait_ge(const_ready, 1)
            pe.wait_ge(vec_landed, 16 * (len(vectors) + 2))
            pe.transpose(ps[:, 7, 0:P], rows[:], ident[:])
            pe.matmul(ps[:, 7, P:2 * P], ident[:, R_GR:R_GR + 1].to_broadcast([P, P]), rows[:],
                      start=True, stop=True).then_inc(rows_turned, 1)

            def turn_norm(i):
                if i == 0:
                    pe.wait_ge(cols_ready, 1)
                for k in range(KD):
                    for t in range(TT):
                        if k == 0:
                            pe.wait_ge(xn_ready, TT * i + t + 1)
                for b in range(KD // 2):
                    for kk in range(2):
                        for t in range(TT):
                            ins = pe.transpose(ps[:, 4 + b, kk * SEQ + t * P:kk * SEQ + (t + 1) * P],
                                               xn[:, t, (2 * b + kk) * P:(2 * b + kk + 1) * P], ident[:])
                    ins.then_inc(xn_turned, 1)

            turn_norm(0)
            for j, g in enumerate(U_WIN):
                use(g)
                for kk in range(2):
                    k = 2 * j + kk
                    pe.wait_ge(act_lo_ready, k + 1)
                    for i in range(TT):
                        for c in range(2):
                            w = CAT // 2
                            ins = product(ps[:, 2 * i + c, 0:w], token_block(k, i),
                                          cols_of(g, kk * CAT + c * w, w), k == 0, k == KD - 1)
                ins.then_inc(unit_used, 1)
            for i in range(TT):
                pe.wait_ge(lat_scaled, 2 * (i + 1))
                for c in range(LAT):
                    ins = pe.transpose(ps[:, 4 + c // 2, c % 2 * SEQ + i * P:c % 2 * SEQ + (i + 1) * P],
                                       hcat[:, i, c * P:(c + 1) * P], ident[:])
            ins.then_inc(lat_turned, 1)
            lat = (lat_hi, lat_lo)
            for j, g in enumerate(U_KV):
                use(g)
                pe.wait_ge(lat_lo_ready, LAT)
                for i in range(TT):
                    for c in range(2):
                        for k in range(KKV):
                            ins = product(ps[:, 4 * j + 2 * i + c, :],
                                          parts(lat, slice(None), KQ + k, slice(i * P, (i + 1) * P)),
                                          cols_of(g, k * 1024 + c * BANK, BANK), k == 0, k == KKV - 1)
                ins.then_inc(unit_used, 1)
            for j, g in enumerate(U_Q):
                use(g)
                for i in range(TT):
                    pe.wait_ge(kv1_copied if j == 1 else kv0_copied, 2 * i + (6 if j == 2 else 2))
                    for k in range(KQ):
                        ins = product(ps[:, 2 * j + i, :],
                                      parts(lat, slice(None), k, slice(i * P, (i + 1) * P)),
                                      cols_of(g, k * BANK, BANK), k == 0, k == KQ - 1)
                ins.then_inc(unit_used, 1)
            pe.wait_ge(kv0_copied, 8)
            pe.wait_ge(kv1_copied, 8)
            pe.wait_ge(q_copied, 6)
            for b in range(12):
                bank = (6 + b) % 8
                pe.wait_ge(kq_normed, 2 if b < 4 else 4 if b < 6 else 6 if b < 10 else 8)
                if b >= 8:
                    pe.wait_ge(kqT_act, b // 2 - 3)
                    pe.wait_ge(kqT_dve, b // 2 - 3)
                for kk in range(2):
                    for i in range(TT):
                        if b < 4:
                            src = kn[:, i, 2 * b + kk, :]
                        elif b < 6:
                            p = 2 * (b - 4) + kk
                            src = kr[:, i, 2 * p:2 * p + 2, :].rearrange("p h d -> p (h d)")
                        elif b < 10:
                            src = qn[:, i, 2 * (b - 6) + kk, 0:NOPE]
                        else:
                            p = 2 * (b - 10) + kk
                            src = qr[:, i, 2 * p:2 * p + 2, :].rearrange("p h d -> p (h d)")
                        ins = pe.transpose(ps[:, bank, kk * SEQ + i * P:kk * SEQ + (i + 1) * P], src, ident[:])
                ins.then_inc(kq_turned, 1)
            pe.wait_ge(kqT_act, 7)
            pe.wait_ge(kqT_dve, 7)

            def scores(h):
                if h >= 2:
                    pe.wait_ge(smax_ready, h - 1)
                for i in range(TT):
                    dst = ps[:, 2 + h % 2, i * P:i * P + (i + 1) * P]
                    pe.matmul(dst, qT[:, h, i * P:(i + 1) * P], kT[:, h, 0:(i + 1) * P],
                              start=True, stop=False)
                    ins = pe.matmul(dst, qrT[:, h, i * P:(i + 1) * P], krT[:, h // 2, 0:(i + 1) * P],
                                    start=False, stop=True)
                ins.then_inc(scores_ready, 1)

            def turn_probs(h):
                pe.wait_ge(probs_ready, 2 * (h + 1))
                if h >= 2:
                    pe.wait_ge(probsT_ready, h - 1)
                for j in range(3):
                    ins = pe.transpose(ps[:, 4 + h % 2, j * P:(j + 1) * P], pr[h % 2][:, j * P:(j + 1) * P],
                                       ident[:])
                ins.then_inc(probs_turned, 1)

            def values(h):
                pe.wait_ge(probsT_ready, h + 1)
                if h >= 2:
                    pe.wait_ge(o_lo_ready, h - 1)
                pe.matmul(ps[:, 6 + h % 2, 0:SEQ], vt[:, 0, h, :], prT[h % 2][:, 0:SEQ],
                          start=True, stop=False)
                pe.matmul(ps[:, 6 + h % 2, P:SEQ], vt[:, 1, h, :], prT[h % 2][:, SEQ:3 * P],
                          start=False, stop=True).then_inc(pv_ready, 1)

            for h in range(HEADS + 2):
                if h < HEADS:
                    scores(h)
                if 1 <= h <= HEADS:
                    turn_probs(h - 1)
                if h >= 2:
                    values(h - 2)

            def into_residual(g, chunk_parts, first, last):
                use(g)
                for kk in range(2):
                    for i in range(TT):
                        a = chunk_parts(kk, i)
                        for c in range(2):
                            ins = product(ps[:, 2 * i + c, :], a, cols_of(g, kk * D + c * BANK, BANK),
                                          first and kk == 0, last and kk == 1)
                ins.then_inc(unit_used, 1)

            for j, g in enumerate(U_WO):
                pe.wait_ge(o_lo_ready, 2 * j + 2)
                into_residual(g, lambda kk, i: token_block(2 * j + kk, i), j == 0, j == 3)

            turn_norm(1)

            def ffn_up(g, s, which):
                use(g)
                for c in range(2):
                    for k in range(KD):
                        if s == 0 and which == 0 and c == 0:
                            pe.wait_ge(act_lo_ready, KD + k + 1)
                        ins = product(ps[:, 4 + 2 * (s % 2) + which, c * SEQ:(c + 1) * SEQ],
                                      cols_of(g, k * 256 + c * P, P), tokens(k), k == 0, k == KD - 1)
                ins.then_inc(unit_used, 1)

            def ffn_down(s):
                pe.wait_ge(f_lo_ready, s + 1)
                if s == 0:
                    pe.wait_ge(res_ready, 4)
                into_residual(U_F2[s], lambda kk, i: (f_hi[:, kk * SEQ + i * P:kk * SEQ + (i + 1) * P],
                                                      f_lo[:, kk * SEQ + i * P:kk * SEQ + (i + 1) * P]),
                              s == 0, s == FSTEPS - 1)

            for s in range(FSTEPS + 1):
                if s < FSTEPS:
                    if s == 0:
                        pe.wait_ge(act_lo_ready, 2 * KD)
                    if s >= 2:
                        pe.wait_ge(f_h_ready, s - 1)
                    ffn_up(U_F1[s], s, 0)
                if s:
                    ffn_down(s - 1)
                if s < FSTEPS:
                    ffn_up(U_F3[s], s, 1)

            turn_norm(2)

            def lru_in(g, s, bank):
                use(g)
                for c in range(2):
                    for k in range(KD):
                        ins = product(ps[:, bank, c * SEQ:(c + 1) * SEQ],
                                      cols_of(g, k * 256 + c * P, P), tokens(k), k == 0, k == KD - 1)
                ins.then_inc(unit_used, 1)

            def lru_out(s):
                pe.wait_ge(y_lo_ready, s + 1)
                if s == 0:
                    pe.wait_ge(res_ready, 8)
                into_residual(U_O[s], lambda kk, i: (lc_hi[:, kk, i * P:(i + 1) * P],
                                                     lc_lo[:, kk, i * P:(i + 1) * P]), s == 0, False)

            def lru_gates(s):
                use(U_GA[s])
                pe.wait_ge(xc_lo_ready, s + 1)
                for a in range(2):
                    for c in range(2):
                        ins = product(ps[:, 6 + a, c * SEQ:(c + 1) * SEQ], cols_of(U_GA[s], a * 256 + c * P, P),
                                      (lc_hi[:, c, :], lc_lo[:, c, :]), True, True)
                ins.then_inc(unit_used, 1)

            for s in range(LSTEPS + 1):
                if s < LSTEPS:
                    if s == 0:
                        pe.wait_ge(act_lo_ready, 3 * KD)
                    else:
                        pe.wait_ge(xb_ready, 2 * s)
                    lru_in(U_X[s], s, 4)
                    if s:
                        pe.wait_ge(gexp_ready, s)
                    lru_in(U_G[s], s, 5)
                if s:
                    lru_out(s - 1)
                if s < LSTEPS:
                    if s:
                        pe.wait_ge(sig_exp, 4 * s)
                    lru_gates(s)
            for i in range(TT):
                for k in range(KD):
                    bias = ident[:, R_BO + k:R_BO + k + 1].to_broadcast([P, P])
                    ins = pe.matmul(ps[:, 2 * i + k // 4, k % 4 * P:(k % 4 + 1) * P], bias, rows[:],
                                    start=False, stop=k % 4 == 3)
            ins.then_inc(gain_rows, 1)

            pe.wait_ge(y_lo_ready, LSTEPS)
            for k in range(KD):
                r = R_FFN + KD + k
                ins = pe.matmul(ps[:, 4 + k // 4, k % 4 * P:(k % 4 + 1) * P],
                                ident[:, r:r + 1].to_broadcast([P, P]), rows[:], start=True, stop=True)
            ins.then_inc(gain_rows, 1)
            pe.wait_ge(rx_ready, 4)
            for b in range(KD // 2):
                for kk in range(2):
                    for i in range(TT):
                        ins = pe.transpose(ps[:, b, kk * SEQ + i * P:kk * SEQ + (i + 1) * P],
                                           rx[:, i, (2 * b + kk) * P:(2 * b + kk + 1) * P], ident[:])
                ins.then_inc(rx_turned, 1)
            pe.wait_ge(small_landed, 32)
            for i in range(TT):
                for k in range(KD):
                    pe.wait_ge(rxT_ready, k // 2 + 1)
                    ins = pe.matmul(ps[:, 6, i * E:(i + 1) * E], rxT[:, k, i * P:(i + 1) * P], w_router[:, k, :],
                                    start=k == 0, stop=k == KD - 1)
            ins.then_inc(logits_ready, 1)
            chosen = rsm[6]
            pe.wait_ge(mask_ready, 1)
            pe.matmul(ps[:, 7, 0:E], before[:], chosen[:, 0, :], start=True, stop=True)
            pe.matmul(ps[:, 7, E:2 * E], ones[:], chosen[:, 0, :], start=True, stop=False)
            pe.matmul(ps[:, 7, E:2 * E], before[:], chosen[:, 1, :], start=False, stop=True)
            pe.matmul(ps[:, 7, 2 * E:3 * E], ones[:], chosen[:, 0, :], start=True, stop=False)
            pe.matmul(ps[:, 7, 2 * E:3 * E], ones[:], chosen[:, 1, :], start=False,
                      stop=True).then_inc(ranks_ready, 1)

            def gather(base):
                pe.wait_ge(sel_ready, base + 2)
                for k in range(KD):
                    for j, src in enumerate((act_hi, act_lo)):
                        for i in range(TT):
                            ins = pe.matmul(ps[:, 2 + k // 4, k % 4 * P:(k % 4 + 1) * P],
                                            src[:, i * D + k * P:i * D + (k + 1) * P], sel[:, i, :],
                                            start=j == 0 and i == 0, stop=j == 1 and i == TT - 1)
                    if k % 4 == 3:
                        ins.then_inc(gathered, 1)

            def scatter(base, number):
                pe.wait_ge(selT_ready, number)
                for i in range(TT):
                    for b in range(2):
                        pe.wait_ge(y_lo_split, base + (b + 1))
                        pe.matmul(ps[:, 2 + 2 * i + b, :], selT[:, i * P:(i + 1) * P], y_hi[:, b * BANK:(b + 1) * BANK],
                                  start=True, stop=False)
                        pe.matmul(ps[:, 2 + 2 * i + b, :], selT[:, i * P:(i + 1) * P], y_lo[:, b * BANK:(b + 1) * BANK],
                                  start=False, stop=True).then_inc(scattered, 1)

            def one_pass(n, e, kind):
                u_base, t_base = held(pe, n * N_BODY), held(pe, n * MSTEPS)
                h_base, s_base = held(pe, n * 2), held(pe, n * 4)
                selT_count = held(pe, n + 1)

                def split(u):
                    pe.wait_ge(lo_ready, u_base + (N_PRE + u + 1))

                def up(table, t, half, bank):
                    u = table[t, half]
                    split(u)
                    for k in range(4):
                        kk = 4 * half + k
                        ins = product(ps[:, bank, :], (in_hi[:, kk * P:(kk + 1) * P], in_lo[:, kk * P:(kk + 1) * P]),
                                      cols_of(N_PRE + u, k * BANK, BANK), kk == 0, kk == KD - 1)
                    ins.then_inc(unit_used, 1)

                def turn(t):
                    pe.wait_ge(h_ready, t_base + (t + 1))
                    for c in range(4):
                        ins = pe.transpose(ps[:, 6, c * P:(c + 1) * P], e_h[t % 2][:, c * P:(c + 1) * P], ident[:])
                    ins.then_inc(h_turned, 1)

                def down(t):
                    pe.wait_ge(hT_lo_ready, t_base + (t + 1))
                    for half in range(2):
                        u = M_W2[t, half]
                        split(u)
                        for k in range(2):
                            c = 2 * half + k
                            for b in range(2):
                                ins = product(ps[:, 4 + b, :], (hT_hi[:, c * P:(c + 1) * P], hT_lo[:, c * P:(c + 1) * P]),
                                              cols_of(N_PRE + u, k * D + b * BANK, BANK),
                                              t == 0 and c == 0, t == MSTEPS - 1 and c == 3)
                        ins.then_inc(unit_used, 1)

                if kind == "extra":
                    pe.wait_ge(res_ready, s_base + (R_PRE + 4))
                    gather(h_base)
                for t in range(MSTEPS):
                    bank = 2 * (t % 2)
                    if t == 0:
                        pe.wait_ge(in_lo_ready, h_base + 1)
                    elif t == 1 and kind != "extra":
                        pe.wait_ge(res_ready, s_base + (R_PRE + 2))
                    up(M_W1, t, 0, bank)
                    if t == 0:
                        pe.wait_ge(in_lo_ready, h_base + 2)
                    up(M_W1, t, 1, bank)
                    if t == 0 and kind != "extra":
                        scatter(h_base, selT_count)
                    if t:
                        turn(t - 1)
                    if t == 1:
                        for i in range(TT):
                            pe.transpose(ps[:, 7, i * P:(i + 1) * P], sel[:, i, :].bitcast(F32), ident[:])
                        for i in range(TT):
                            ins = pe.matmul(ps[:, 7, SEQ:SEQ + 1], sel[:, i, :].bitcast(F32), gates[:, i, bass.ds(e, 1)],
                                            start=i == 0, stop=i == TT - 1)
                        ins.then_inc(selT_turned, 1)
                    up(M_W3, t, 0, bank + 1)
                    up(M_W3, t, 1, bank + 1)
                    if t == 1 and kind != "extra":
                        pe.wait_ge(res_ready, s_base + (R_PRE + 4))
                    if t:
                        down(t - 1)
                turn(MSTEPS - 1)
                if kind == "next":
                    gather(h_base + 2)
                down(MSTEPS - 1)
                if kind != "next":
                    scatter(h_base + 2, selT_count + 1)

            def first_tokens():
                pe.wait_ge(y_zeroed, 1)
                gather(0)

            experts(pe, lambda n, e, off: one_pass(n, e, "next"), first_tokens,
                    lambda n, e, off: one_pass(n, e, "last"), lambda n, e, off: one_pass(n, e, "extra"))

        @block.scalar
        def _(act):
            own = Chain(act, act_own)

            def hi(g):
                act.wait_ge(raw_landed[slot_of(g)], landed_at[g])
                if g >= SPLIT_SLOTS:
                    act.wait_ge(unit_used, g - SPLIT_SLOTS + 1)
                act.activation(w_hi[g % SPLIT_SLOTS][:, 0:width[g]], raw[slot_of(g)][:, 0:width[g]],
                               ACT.Copy).then_inc(hi_ready, 1)

            for r, src in vectors:
                act.dma_start(rows[r:r + src.shape[0], :], src).then_inc(vec_landed, 16)
            act.dma_start(rows[R_GR:R_GR + 1, 0:ROPE], mla_g_qn[:, NOPE:QK_HEAD]).then_inc(vec_landed, 16)
            act.dma_start(rows[R_GR:R_GR + 1, ROPE:2 * ROPE], mla_g_kn[:, NOPE:QK_HEAD]).then_inc(vec_landed, 16)
            with nc.allow_non_contiguous_dma(reason="256 positions, one per token"):
                act.dma_start(pos_i[:], positions[0].rearrange("(i p) -> p i", p=P)).then_inc(pos_landed, 16)
            act.dma_start(freq[:], inv_freq.partition_broadcast(P)).then_inc(pos_landed, 16)
            act.dma_start(w_router[:], moe_w_router[0].rearrange("(k p) e -> p k e", p=P)).then_inc(small_landed, 16)
            act.dma_start(b_router[:], moe_b_router[0].partition_broadcast(P)).then_inc(small_landed, 16)

            def norm_squares(i):
                if i == 0:
                    act.wait_ge(x_landed, 16 * TT)
                else:
                    act.wait_ge(res_ready, 4 * i)
                act.activation(xn[:, 0, :], res[:, 0, :], ACT.Square, accum_out=sumsq[:, 0:1]).then_inc(sq_act, 1)

            def norm_hi(i, gain):
                for k in range(KD):
                    act.wait_ge(xn_turned, 4 * i + k // 2 + 1)
                    act.activation(act_hi[:, k * SEQ:(k + 1) * SEQ], ps[:, 4 + k // 2, k % 2 * SEQ:(k % 2 + 1) * SEQ],
                                   ACT.Copy, scale=cols[:, gain + k:gain + k + 1]).then_inc(act_hi_ready, 1)

            norm_squares(0)
            for g in range(3):
                hi(g)
            act.wait_ge(pos_landed, 32)
            act.wait_ge(cols_ready, 2)
            act.activation(sin[:], trig[2][:], ACT.Sin).then_inc(trig_ready, 1)
            act.activation(cos[:], trig[3][:], ACT.Sin).then_inc(trig_ready, 1)
            act.wait_ge(cols_ready, 1)
            norm_hi(0, R_MIX)
            for g in range(3, 7):
                hi(g)
            for i in range(TT):
                for c in range(2):
                    w = CAT // 2
                    act.activation(hcat[:, i, c * w:(c + 1) * w], ps[:, 2 * i + c, 0:w], ACT.Copy).then_inc(cat_ready, 1)
            act.wait_ge(cat_ready, 2 * TT)
            for i in range(TT):
                cat_junk = junk[:, i * 1024:(i + 1) * 1024]
                act.activation(cat_junk[:, 0:Q_LORA], hcat[:, i, 0:Q_LORA], ACT.Square,
                               accum_out=sumsq[:, 2 + i:3 + i]).then_inc(cat_sq, 1)
                act.activation(cat_junk[:, Q_LORA:Q_LORA + KV_LORA], hcat[:, i, Q_LORA:Q_LORA + KV_LORA], ACT.Square,
                               accum_out=sumsq[:, 4 + i:5 + i]).then_inc(cat_sq, 1)
            for c in range(LAT):
                act.wait_ge(lat_turned, 1)
                act.activation(lat_hi[:, c, :], ps[:, 4 + c // 2, c % 2 * SEQ:(c % 2 + 1) * SEQ], ACT.Copy,
                               scale=cols[:, R_QA + c:R_QA + c + 1]).then_inc(lat_hi_ready, 1)
            hi(7)

            def copy_kv(j):
                for c in range(2):
                    src = ps[:, 4 * j + c, :].rearrange("p (h d) -> p h d", h=2)
                    h = 4 * j + 2 * c
                    act.activation(kn[:, 0, h:h + 2, :], src[:, :, 0:NOPE], ACT.Copy).then_inc(kv0_copied, 1)
                    act.activation(vt[:, 0, h:h + 2, :], src[:, :, NOPE:], ACT.Copy).then_inc(kv0_copied, 1)

            copy_kv(0)
            hi(8)
            copy_kv(1)
            for j in range(3):
                hi(9 + j)
                for i in range(TT):
                    q_flat = qn[:, i, :, :].rearrange("p h d -> p (h d)")
                    act.activation(q_flat[:, j * BANK:(j + 1) * BANK], ps[:, 2 * j + i, :],
                                   ACT.Copy).then_inc(q_copied, 1)
            act.wait_ge(const_ready, 2)
            for b in range(0, 12, 2):
                bank = (6 + b) % 8
                act.wait_ge(kq_turned, b + 1)
                src = ps[:, bank, :].rearrange("p (a t) -> p a t", a=2)
                if b < 4:
                    act.activation(kT[:, 2 * b:2 * b + 2, :], src, ACT.Copy,
                                   scale=cols[:, R_KN:R_KN + 1]).then_inc(kqT_act, 1)
                elif b < 6:
                    act.activation(krT[:, 2 * (b - 4):2 * (b - 4) + 2, :], src, ACT.Copy).then_inc(kqT_act, 1)
                elif b < 10:
                    act.activation(qT[:, 2 * (b - 6):2 * (b - 6) + 2, :], src, ACT.Copy,
                                   scale=cols[:, R_QN:R_QN + 1]).then_inc(kqT_act, 1)
                else:
                    h = 4 * (b - 10)
                    act.activation(qrT[0:ROPE, h:h + 4:2, :], src[0:ROPE], ACT.Copy).then_inc(kqT_act, 1)
                    act.activation(qrT[ROPE:P, h + 1:h + 4:2, :], src[ROPE:P], ACT.Copy).then_inc(kqT_act, 1)

            def exps(h):
                act.wait_ge(smax_ready, h + 1)
                if h >= 2:
                    act.wait_ge(probs_turned, h - 1)
                for i in range(TT):
                    at = slice(i * P, i * P + (i + 1) * P)
                    act.activation(pr[h % 2][:, at], sc[h % 2][:, at], ACT.Exp, bias=smax[:, h, i:i + 1],
                                   accum_out=ssum[:, h, i:i + 1]).then_inc(exp_ready, 1)

            def probs_T(h):
                act.wait_ge(probs_turned, h + 1)
                if h >= 2:
                    act.wait_ge(pv_ready, h - 1)
                act.activation(prT[h % 2][:], ps[:, 4 + h % 2, 0:3 * P], ACT.Copy).then_inc(probsT_ready, 1)

            def head_hi(h):
                act.wait_ge(pv_ready, h + 1)
                act.activation(act_hi[:, h * SEQ:(h + 1) * SEQ], ps[:, 6 + h % 2, 0:SEQ],
                               ACT.Copy).then_inc(o_hi_ready, 1)

            for h in range(HEADS + 2):
                if h < HEADS:
                    exps(h)
                if 1 <= h <= HEADS:
                    probs_T(h - 1)
                if h >= 2:
                    head_hi(h - 2)
            for g in range(12, 16):
                hi(g)

            norm_squares(1)
            norm_hi(1, R_FFN)

            def f_gate(s):
                b = 4 + 2 * (s % 2)
                act.wait_ge(unit_used, U_F1[s] + 1)
                act.activation(f_h[s % 2][:], ps[:, b, :], ACT.Silu).then_inc(f_silu, 1)

            def f_split(s):
                act.wait_ge(f_h_ready, s + 1)
                act.activation(f_hi[:], f_h[s % 2][:], ACT.Copy).then_inc(f_hi_ready, 1)

            hi(N_ATT + 3)
            f_gate(0)
            hi(N_ATT + 4)
            f_split(0)
            for s in range(1, FSTEPS):
                hi(U_F1[s] + 3)
                f_gate(s)
                hi(U_F1[s] + 4)
                f_split(s)
                hi(U_F1[s] + 5)

            act.wait_ge(lam_ready, 1)
            act.activation(lam[1][:], lam[0][:], ACT.Exp).then_inc(lam_exp, 1)
            norm_squares(2)
            norm_hi(2, R_MIX + KD)

            def x_work(s):
                act.wait_ge(unit_used, U_X[s] + 1)
                if s:
                    act.wait_ge(conv_ready, 2 * s)
                for c in range(2):
                    b = R_BIN + KD + 2 * s + c
                    act.activation(xpad[:, c, 3:3 + SEQ], ps[:, 4, c * SEQ:(c + 1) * SEQ], ACT.Identity,
                                   bias=cols[:, b:b + 1]).then_inc(xb_ready, 1)
                if s == 0:
                    conv_hi(0)

            def conv_hi(s):
                act.wait_ge(conv_ready, 2 * (s + 1))
                if s:
                    act.wait_ge(unit_used, U_O[s - 1] + 1)
                act.activation(lc_hi[:], xc[:], ACT.Copy).then_inc(xc_hi_ready, 1)

            def g_work(s):
                act.wait_ge(gin_ready, s + 1)
                act.activation(tm[:], tm[:], ACT.Exp).then_inc(gexp_ready, 1)

            def a_work(s):
                act.wait_ge(unit_used, U_GA[s] + 1)
                for a, dst in enumerate((ra, iu)):
                    for c in range(2):
                        act.activation(dst[:, c, :], ps[:, 6 + a, c * SEQ:(c + 1) * SEQ], ACT.Exp, scale=-1.0,
                                       bias=bias_n[:, a, 2 * s + c:2 * s + c + 1]).then_inc(sig_exp, 1)
                act.wait_ge(sig_ready, 2 * (s + 1))
                for c in range(2):
                    h = 2 * s + c
                    act.activation(tm[:, c, :], ra[:, c, :], ACT.Tanh, scale=decay[:, 0, h:h + 1]).then_inc(at_ready, 1)
                for c in range(2):
                    h = 2 * s + c
                    act.activation(ra[:, c, :], ra[:, c, :], ACT.Exp, scale=decay[:, 1, h:h + 1]).then_inc(at_ready, 1)
                act.wait_ge(v_ready, s + 1)
                act.activation(tm[:], tm[:], ACT.Sqrt).then_inc(mult_ready, 1)
                act.wait_ge(y_ready, s + 1)
                act.activation(lc_hi[:], xc[:], ACT.Copy).then_inc(y_hi_ready, 1)

            lru_order(hi, x_work, g_work, a_work, conv_hi)

            norm_squares(3)
            for i in range(TT):
                act.wait_ge(rx_ready, 2 * (i + 1))
                act.activation(act_hi[:, i * D:(i + 1) * D], rx[:, i, :], ACT.Copy).then_inc(tok_hi_ready, 1)
            for b in range(KD // 2):
                act.wait_ge(rx_turned, b + 1)
                act.activation(rxT[:, 2 * b:2 * b + 2, :], ps[:, b, :].rearrange("p (k t) -> p k t", k=2),
                               ACT.Copy).then_inc(rxT_ready, 1)
            act.wait_ge(top_ready, 1)
            act.activation(rsm[3][:, :, 0:1], rsm[2][:, :, 0:1], ACT.Exp).then_inc(top_exp, 1)
            act.wait_ge(routed, 1)

            def take_in(base):
                for b in range(2):
                    act.wait_ge(gathered, base + (b + 1))
                    act.activation(in_hi[:, b * BANK:(b + 1) * BANK], ps[:, 2 + b, :], ACT.Copy).then_inc(in_hi_ready, 1)

            def hi_of(u_base, l_base, u):
                slot = slot_of(N_PRE + u)
                landed = slot_count[slot] + 16 * (u // RAW_SLOTS + 1)
                act.wait_ge(raw_landed[slot], l_base + landed)
                act.wait_ge(unit_used, u_base + (N_PRE + u - SPLIT_SLOTS + 1))
                act.activation(w_hi[(N_PRE + u) % SPLIT_SLOTS][:], raw[slot][:], ACT.Copy).then_inc(hi_ready, 1)

            def one_pass(n, kind):
                u_base, t_base = held(act, n * N_BODY), held(act, n * MSTEPS)
                h_base, l_base = held(act, n * 2), held(act, n * (16 * OCC))

                def silu(t):
                    act.wait_ge(unit_used, u_base + (N_PRE + M_W1[t, 1] + 1))
                    if t == 0 and kind != "extra":
                        act.wait_ge(scattered, n * 4 + 4)
                    act.activation(e_h[t % 2][:], ps[:, 2 * (t % 2), :], ACT.Silu).then_inc(silu_ready, 1)

                def turned(t):
                    act.wait_ge(h_turned, t_base + (t + 1))
                    act.activation(hT_hi[:], ps[:, 6, :], ACT.Copy).then_inc(hT_hi_ready, 1)

                if kind == "extra":
                    hi_of(u_base, l_base, 0)
                    take_in(h_base)
                    hi_of(u_base, l_base, 1)
                    hi_of(u_base, l_base, 2)
                for u in range(3, N_BODY):
                    hi_of(u_base, l_base, u)
                    for t in range(MSTEPS):
                        if u == M_W1[t, 1] + 3:
                            silu(t)
                            if t:
                                turned(t - 1)
                            if t == 1:
                                act.wait_ge(selT_turned, n + 1)
                                act.activation(selT[:], ps[:, 7, 0:SEQ], ACT.Copy).then_inc(selT_ready, 1)
                                act.activation(slot_gate[:], ps[:, 7, SEQ:SEQ + 1], ACT.Copy).then_inc(gate_col_ready, 1)
                turned(MSTEPS - 1)
                if kind == "next":
                    take_in(h_base + 2)
                    for u in range(3):
                        hi_of(u_base, l_base, N_BODY + u)
                act.wait_ge(unit_used, u_base + (N_PRE + N_BODY))
                act.wait_ge(gate_col_ready, n + 1)
                for b in range(2):
                    act.activation(y_hi[:, b * BANK:(b + 1) * BANK], ps[:, 4 + b, :], ACT.Copy,
                                   scale=slot_gate[:, 0:1]).then_inc(out_hi_ready, 1)

            def first_tokens():
                act.activation(selT[:], slot_ids[:], ACT.Copy, scale=0.0).then_inc(selT_ready, 1)
                take_in(0)
                for u in range(3):
                    hi_of(0, 0, u)

            experts(act, lambda n, e, off: one_pass(n, "next"), first_tokens,
                    lambda n, e, off: one_pass(n, "last"), lambda n, e, off: one_pass(n, "extra"))

        @block.vector
        def _(dve):
            own = Chain(dve, dve_own)

            def lo(g):
                dve.wait_ge(hi_ready, g + 1)
                s, w = g % SPLIT_SLOTS, width[g]
                dve.tensor_tensor(w_lo[s][:, 0:w], raw[slot_of(g)][:, 0:w], w_hi[s][:, 0:w].bitcast(F32),
                                  ALU.subtract).then_inc(lo_ready, 1)

            def norm_scale(i):
                if i == 0:
                    dve.wait_ge(x_landed, 16 * TT)
                else:
                    dve.wait_ge(res_ready, 4 * i)
                dve.tensor_tensor_reduce(xn[:, 1, :], res[:, 1, :], res[:, 1, :], 1.0, 0.0, ALU.mult, ALU.add,
                                         sumsq[:, 1:2]).then_inc(sq_dve, 1)

            def norm_apply(i):
                dve.wait_ge(rstd_ready, i + 1)
                for t in range(TT):
                    dve.tensor_scalar(xn[:, t, :], res[:, t, :], rstd[:, t:t + 1], None, ALU.mult).then_inc(xn_ready, 1)

            def norm_lo(i, gain):
                for k in range(KD):
                    dve.wait_ge(act_hi_ready, KD * i + k // 2 * 2 + 2)
                    at = slice(k * SEQ, (k + 1) * SEQ)
                    dve.scalar_tensor_tensor(out=act_lo[:, at], in0=ps[:, 4 + k // 2, k % 2 * SEQ:(k % 2 + 1) * SEQ],
                                             scalar=cols[:, gain + k:gain + k + 1], in1=act_hi[:, at].bitcast(F32),
                                             op0=ALU.mult, op1=ALU.subtract).then_inc(act_lo_ready, 1)

            norm_scale(0)
            dve.wait_ge(rows_turned, 1)
            own.step(dve.tensor_copy(g_rope[:], ps[:, 7, P:2 * P]))
            own.step(dve.tensor_copy(cols[:], ps[:, 7, 0:P]))
            own.settle()
            dve.tensor_scalar(bias_n[:].rearrange("p a h -> p (a h)"), cols[:, R_BA:R_BA + 16], -1.0, None,
                              ALU.mult).then_inc(cols_ready, 1)
            dve.wait_ge(pos_landed, 32)
            posf, turns, red, halfr = trig
            own.link(dve.tensor_copy(ssr[:], pos_i[:]))
            for i in range(TT):
                own.step(dve.tensor_scalar(posf[:, i, :], freq[:], ssr[:, i:i + 1], None, ALU.mult))
            own.settle()
            own.link(dve.tensor_scalar(turns[:], posf[:], 1.0 / (2 * np.pi), ROUND_MAGIC, ALU.mult, ALU.add))
            own.link(dve.tensor_scalar(turns[:], turns[:], -ROUND_MAGIC, None, ALU.add))
            own.link(dve.scalar_tensor_tensor(out=red[:], in0=turns[:], scalar=-TWO_PI_A, in1=posf[:],
                                              op0=ALU.mult, op1=ALU.add))
            own.link(dve.scalar_tensor_tensor(out=red[:], in0=turns[:], scalar=-TWO_PI_B, in1=red[:],
                                              op0=ALU.mult, op1=ALU.add))
            own.link(dve.scalar_tensor_tensor(out=red[:], in0=turns[:], scalar=-TWO_PI_C, in1=red[:],
                                              op0=ALU.mult, op1=ALU.add))
            own.link(dve.tensor_scalar(red[:], red[:], -PI_FLOOR, PI_FLOOR, ALU.max, ALU.min))
            dve.tensor_scalar(halfr[:], red[:], 0.5, None, ALU.mult).then_inc(cols_ready, 1)
            for g in range(3):
                lo(g)
            norm_apply(0)
            dve.wait_ge(trig_ready, 2)
            own.link(dve.tensor_tensor(cos[:], cos[:], cos[:], ALU.mult))
            own.step(dve.tensor_scalar(cos[:], cos[:], -2.0, 1.0, ALU.mult, ALU.add))
            norm_lo(0, R_MIX)
            for g in range(3, 7):
                lo(g)
            rope_junk = junk[:, Q_LORA + KV_LORA:]
            dve.wait_ge(cat_ready, 2 * TT)
            for i in range(TT):
                own.step(dve.tensor_tensor_reduce(rope_junk[:, i * ROPE:(i + 1) * ROPE], hcat[:, i, CAT - ROPE:], hcat[:, i, CAT - ROPE:],
                                                  1.0, 0.0, ALU.mult, ALU.add, ssr[:, i:i + 1]))
            own.settle()
            dve.wait_ge(lat_rstd, 1)
            for i in range(TT):
                dve.tensor_scalar(hcat[:, i, 0:Q_LORA], hcat[:, i, 0:Q_LORA], rstd[:, 2 + i:3 + i], None,
                                  ALU.mult).then_inc(lat_scaled, 1)
                dve.tensor_scalar(hcat[:, i, Q_LORA:Q_LORA + KV_LORA], hcat[:, i, Q_LORA:Q_LORA + KV_LORA],
                                  rstd[:, 4 + i:5 + i], None, ALU.mult).then_inc(lat_scaled, 1)
            for c in range(LAT):
                dve.wait_ge(lat_hi_ready, min(c // 2 * 2 + 2, LAT))
                dve.scalar_tensor_tensor(out=lat_lo[:, c, :], in0=ps[:, 4 + c // 2, c % 2 * SEQ:(c % 2 + 1) * SEQ],
                                         scalar=cols[:, R_QA + c:R_QA + c + 1], in1=lat_hi[:, c, :].bitcast(F32),
                                         op0=ALU.mult, op1=ALU.subtract).then_inc(lat_lo_ready, 1)

            def rope(x1, x2, o1, o2, shape, done=None):
                t = [r[:][tuple(slice(0, n) for n in shape)] for r in rope_t]
                c = cos[:].unsqueeze(2).to_broadcast(shape)
                s = sin[:].unsqueeze(2).to_broadcast(shape)
                for dst, a, b in ((t[0], x1, c), (t[1], x2, s), (t[2], x1, s), (t[3], x2, c)):
                    own.step(dve.tensor_tensor(dst, a, b, ALU.mult))
                own.settle()
                for ins in (dve.tensor_tensor(o1, t[0], t[1], ALU.subtract),
                            dve.tensor_tensor(o2, t[2], t[3], ALU.add)):
                    ins.then_inc(done, 1) if done else own.step(ins)
                own.settle()

            kshape = [P, TT, 1, HALF]
            krope = hcat[:, :, CAT - ROPE:].unsqueeze(2)
            own.link(dve.tensor_tensor(krope, krope, g_rope[:, ROPE:].unsqueeze(1).unsqueeze(1).to_broadcast([P, TT, 1, ROPE]),
                                       ALU.mult))
            rope(krope[:, :, :, 0:HALF], krope[:, :, :, HALF:], krope[:, :, :, 0:HALF], krope[:, :, :, HALF:], kshape)
            lo(7)

            def copy_kv(j):
                dve.wait_ge(unit_used, U_KV[j] + 1)
                for c in range(2):
                    src = ps[:, 4 * j + 2 + c, :].rearrange("p (h d) -> p h d", h=2)
                    h = 4 * j + 2 * c
                    dve.tensor_copy(kn[:, 1, h:h + 2, :], src[:, :, 0:NOPE]).then_inc(kv1_copied, 1)
                    dve.tensor_copy(vt[:, 1, h:h + 2, :], src[:, :, NOPE:]).then_inc(kv1_copied, 1)

            copy_kv(0)
            lo(8)
            copy_kv(1)
            lo(9)
            dve.wait_ge(kv0_copied, 8)
            dve.wait_ge(kv1_copied, 8)
            for i in range(TT):
                if i:
                    dve.wait_ge(head_sq, HEADS)
                for h in range(HEADS):
                    dve.tensor_tensor_reduce(junk[:, h * NOPE:(h + 1) * NOPE], kn[:, i, h, :], kn[:, i, h, :], 1.0,
                                             ssr[:, i:i + 1], ALU.mult, ALU.add,
                                             ssh[:, 0, i * HEADS + h:i * HEADS + h + 1]).then_inc(head_sq, 1)
            lo(10)
            lo(11)
            dve.wait_ge(q_copied, 6)
            for i in range(TT):
                dve.wait_ge(head_sq, (2 + i) * HEADS)
                for h in range(HEADS):
                    dve.tensor_tensor_reduce(junk[:, h * QK_HEAD:(h + 1) * QK_HEAD], qn[:, i, h, :], qn[:, i, h, :], 1.0,
                                             0.0, ALU.mult, ALU.add,
                                             ssh[:, 1, i * HEADS + h:i * HEADS + h + 1]).then_inc(head_sq, 1)
            dve.wait_ge(head_rstd, 1)
            k_scale = rsh[:, 0, :].rearrange("p (i h) -> p i h", h=HEADS).unsqueeze(3)
            for i in range(TT):
                dve.tensor_tensor(kn[:, i], kn[:, i], k_scale[:, i].to_broadcast([P, HEADS, NOPE]),
                                  ALU.mult).then_inc(kq_normed, 1)
            for i in range(TT):
                dve.tensor_tensor(kr[:, i], krope[:, i].to_broadcast([P, HEADS, ROPE]),
                                  k_scale[:, i].to_broadcast([P, HEADS, ROPE]), ALU.mult).then_inc(kq_normed, 1)
            dve.wait_ge(head_rstd, 2)
            q_scale = rsh[:, 1, :].rearrange("p (i h) -> p i h", h=HEADS).unsqueeze(3)
            for i in range(TT):
                dve.tensor_tensor(qn[:, i], qn[:, i], q_scale[:, i].to_broadcast([P, HEADS, QK_HEAD]),
                                  ALU.mult).then_inc(kq_normed, 1)
            dve.wait_ge(kq_normed, 6)
            for i in range(TT):
                own.step(dve.tensor_tensor(qn[:, i, :, NOPE:], qn[:, i, :, NOPE:],
                                           g_rope[:, 0:ROPE].unsqueeze(1).to_broadcast([P, HEADS, ROPE]), ALU.mult))
            own.settle()
            qshape = [P, TT, HEADS, HALF]
            rope(qn[:, :, :, NOPE:NOPE + HALF], qn[:, :, :, NOPE + HALF:], qr[:, :, :, 0:HALF], qr[:, :, :, HALF:], qshape,
                 kq_normed)
            for b in range(1, 12, 2):
                bank = (6 + b) % 8
                dve.wait_ge(kq_turned, b + 1)
                src = ps[:, bank, :].rearrange("p (a t) -> p a t", a=2)
                if b < 4:
                    dve.tensor_scalar(kT[:, 2 * b:2 * b + 2, :], src, cols[:, R_KN:R_KN + 1], None,
                                      ALU.mult).then_inc(kqT_dve, 1)
                elif b < 6:
                    dve.tensor_copy(krT[:, 2 * (b - 4):2 * (b - 4) + 2, :], src).then_inc(kqT_dve, 1)
                elif b < 10:
                    dve.tensor_scalar(qT[:, 2 * (b - 6):2 * (b - 6) + 2, :], src, cols[:, R_QN:R_QN + 1], None,
                                      ALU.mult).then_inc(kqT_dve, 1)
                else:
                    h = 4 * (b - 10)
                    dve.tensor_copy(qrT[0:ROPE, h:h + 4:2, :], src[0:ROPE]).then_inc(kqT_dve, 1)
                    dve.tensor_copy(qrT[ROPE:P, h + 1:h + 4:2, :], src[ROPE:P]).then_inc(kqT_dve, 1)

            def score_max(h):
                dve.wait_ge(scores_ready, h + 1)
                if h >= 2:
                    dve.wait_ge(exp_ready, 2 * (h - 1))
                s = sc[h % 2]
                own.link(dve.tensor_tensor(s[:], ps[:, 2 + h % 2, 0:3 * P], mask[:], ALU.add))
                for i in range(TT):
                    own.step(dve.tensor_reduce(smax[:, h, i:i + 1], s[:, i * P:i * P + (i + 1) * P], AX.X, ALU.max))
                own.settle()
                dve.tensor_scalar(smax[:, h, :], smax[:, h, :], -1.0, None, ALU.mult).then_inc(smax_ready, 1)

            def normalise(h):
                dve.wait_ge(exp_ready, 2 * h + 2)
                own.link(dve.reciprocal(sinv[:, h, :], ssum[:, h, :]))
                for i in range(TT):
                    at = slice(i * P, i * P + (i + 1) * P)
                    dve.tensor_scalar(pr[h % 2][:, at], pr[h % 2][:, at], sinv[:, h, i:i + 1], None,
                                      ALU.mult).then_inc(probs_ready, 1)

            def head_lo(h):
                dve.wait_ge(o_hi_ready, h + 1)
                at = slice(h * SEQ, (h + 1) * SEQ)
                dve.tensor_tensor(act_lo[:, at], ps[:, 6 + h % 2, 0:SEQ], act_hi[:, at].bitcast(F32),
                                  ALU.subtract).then_inc(o_lo_ready, 1)

            for h in range(HEADS + 2):
                if h < HEADS:
                    score_max(h)
                if 1 <= h <= HEADS:
                    normalise(h - 1)
                if h >= 2:
                    head_lo(h - 2)

            def add_residual(last_unit, i0, extra=None):
                dve.wait_ge(unit_used, last_unit + 1)
                if extra:
                    dve.wait_ge(*extra)
                for i in range(TT):
                    for c in range(2):
                        at = slice(c * BANK, (c + 1) * BANK)
                        dve.tensor_tensor(res[:, i, at], res[:, i, at], ps[:, 2 * i + c, :], ALU.add).then_inc(res_ready, 1)

            for g in range(12, 16):
                lo(g)
            add_residual(U_WO[-1], 0)

            norm_scale(1)
            norm_apply(1)
            norm_lo(1, R_FFN)

            def f_mult(s):
                b = 4 + 2 * (s % 2)
                h = f_h[s % 2][:]
                dve.wait_ge(unit_used, U_F3[s] + 1)
                dve.wait_ge(f_silu, s + 1)
                dve.tensor_tensor(h, h, ps[:, b + 1, :], ALU.mult).then_inc(f_h_ready, 1)
                dve.wait_ge(f_hi_ready, s + 1)
                dve.tensor_tensor(f_lo[:], f_h[s % 2][:], f_hi[:].bitcast(F32), ALU.subtract).then_inc(f_lo_ready, 1)

            lo(N_ATT + 3)
            f_mult(0)
            lo(N_ATT + 4)
            for s in range(1, FSTEPS):
                lo(U_F1[s] + 3)
                lo(U_F1[s] + 4)
                f_mult(s)
                lo(U_F1[s] + 5)
            add_residual(U_F2[FSTEPS - 1], 4)

            norm_scale(2)
            absl, z, d, w, w2, acc = lam
            lam_cols = cols[:, R_LAM:R_LAM + LRU_HEADS]
            own.link(dve.tensor_scalar(d[:], lam_cols, -1.0, None, ALU.mult))
            dve.tensor_tensor(absl[:], lam_cols, d[:], ALU.min).then_inc(lam_ready, 1)
            norm_apply(2)
            norm_lo(2, R_MIX + KD)
            own.link(dve.memset(xpad[:, :, 0:3], 0.0))

            def x_work(s):
                dve.wait_ge(xb_ready, 2 * (s + 1))
                if s:
                    dve.wait_ge(y_lo_ready, s)
                for c in range(2):
                    h = 2 * s + c

                    def tap(j):
                        return cols[:, R_CW + j * KD + h:R_CW + j * KD + h + 1]

                    own.step(dve.tensor_scalar(xc[:, c, :], xpad[:, c, 0:SEQ], tap(0), cols[:, R_CB + h:R_CB + h + 1],
                                               ALU.mult, ALU.add))
                own.settle()
                for j in range(1, 4):
                    for c in range(2):
                        h = 2 * s + c
                        w_j = cols[:, R_CW + j * KD + h:R_CW + j * KD + h + 1]
                        ins = dve.scalar_tensor_tensor(out=xc[:, c, :], in0=xpad[:, c, j:j + SEQ], scalar=w_j,
                                                       in1=xc[:, c, :], op0=ALU.mult, op1=ALU.add)
                        ins.then_inc(conv_ready, 1) if j == 3 else own.step(ins)
                    own.settle()
                if s == 0:
                    conv_lo(0)

            def conv_lo(s):
                dve.wait_ge(xc_hi_ready, s + 1)
                dve.tensor_tensor(lc_lo[:], xc[:], lc_hi[:].bitcast(F32), ALU.subtract).then_inc(xc_lo_ready, 1)

            def g_work(s):
                c2 = 2.0 * float(np.sqrt(2.0 / np.pi))
                dve.wait_ge(unit_used, U_G[s] + 1)
                if s:
                    dve.wait_ge(y_lo_ready, s)
                for c in range(2):
                    b = R_BIN + 2 * s + c
                    own.step(dve.tensor_scalar(gate[:, c, :], ps[:, 5, c * SEQ:(c + 1) * SEQ], cols[:, b:b + 1], None, ALU.add))
                own.settle()
                own.link(dve.tensor_tensor(tm[:], gate[:], gate[:], ALU.mult))
                own.link(dve.tensor_scalar(tm[:], tm[:], -0.044715 * c2, -c2, ALU.mult, ALU.add))
                dve.tensor_tensor(tm[:], tm[:], gate[:], ALU.mult).then_inc(gin_ready, 1)
                dve.wait_ge(gexp_ready, s + 1)
                own.link(dve.tensor_scalar(tm[:], tm[:], 1.0, None, ALU.add))
                own.link(dve.reciprocal(tm[:], tm[:]))
                own.link(dve.tensor_tensor(gate[:], gate[:], tm[:], ALU.mult))

            def a_work(s):
                dve.wait_ge(sig_exp, 4 * (s + 1))
                for dst in (ra, iu):
                    own.step(dve.tensor_scalar(dst[:], dst[:], 1.0, None, ALU.add))
                own.settle()
                dve.reciprocal(ra[:], ra[:]).then_inc(sig_ready, 1)
                dve.reciprocal(iu[:], iu[:]).then_inc(sig_ready, 1)
                dve.wait_ge(sig_ready, 2 * (s + 1))
                own.link(dve.tensor_tensor(iu[:], iu[:], xc[:], ALU.mult))
                dve.wait_ge(at_ready, 4 * s + 4)
                own.link(dve.tensor_scalar(xc[:], tm[:], 1.0, None, ALU.add))
                own.link(dve.reciprocal(xc[:], xc[:]))
                dve.scalar_tensor_tensor(out=tm[:], in0=tm[:], scalar=2.0, in1=xc[:], op0=ALU.mult,
                                         op1=ALU.mult).then_inc(v_ready, 1)
                dve.wait_ge(mult_ready, s + 1)
                own.link(dve.tensor_tensor(iu[:], iu[:], tm[:], ALU.mult))
                for c in range(2):
                    own.step(dve.tensor_tensor_scan(xc[:, c, :], ra[:, c, :], iu[:, c, :], 0.0, ALU.mult, ALU.add))
                own.settle()
                dve.tensor_tensor(xc[:], xc[:], gate[:], ALU.mult).then_inc(y_ready, 1)
                dve.wait_ge(y_hi_ready, s + 1)
                dve.tensor_tensor(lc_lo[:], xc[:], lc_hi[:].bitcast(F32), ALU.subtract).then_inc(y_lo_ready, 1)

            dve.wait_ge(lam_exp, 1)
            own.link(dve.tensor_scalar(d[:], z[:], 2.0, None, ALU.add))
            own.link(dve.reciprocal(d[:], d[:]))
            own.link(dve.tensor_tensor(w[:], z[:], d[:], ALU.mult))
            own.link(dve.tensor_tensor(w2[:], w[:], w[:], ALU.mult))
            own.link(dve.memset(acc[:], 2.0 / 19))
            for k in range(17, 0, -2):
                own.link(dve.tensor_tensor(acc[:], acc[:], w2[:], ALU.mult))
                own.link(dve.tensor_scalar(acc[:], acc[:], 2.0 / k, None, ALU.add))
            own.link(dve.tensor_tensor(acc[:], acc[:], w[:], ALU.mult))
            own.link(dve.tensor_scalar(d[:], cols[:, R_LAM:R_LAM + LRU_HEADS], 0.0, None, ALU.min))
            own.link(dve.tensor_tensor(d[:], d[:], acc[:], ALU.subtract))
            own.step(dve.tensor_scalar(decay[:, 0, :], d[:], -8.0, None, ALU.mult))
            own.link(dve.tensor_scalar(decay[:, 1, :], d[:], 8.0, None, ALU.mult))
            lru_order(lo, x_work, g_work, a_work, conv_lo)
            add_residual(U_O[LSTEPS - 1], 8, (gain_rows, 1))

            norm_scale(3)
            dve.wait_ge(rstd_ready, 4)
            dve.wait_ge(gain_rows, 2)
            for i in range(TT):
                for c in range(2):
                    at = slice(c * BANK, (c + 1) * BANK)
                    dve.scalar_tensor_tensor(out=rx[:, i, at], in0=res[:, i, at], scalar=rstd[:, i:i + 1],
                                             in1=ps[:, 4 + c, :], op0=ALU.mult, op1=ALU.mult).then_inc(rx_ready, 1)
            for i in range(TT):
                dve.wait_ge(tok_hi_ready, i + 1)
                at = slice(i * D, (i + 1) * D)
                dve.tensor_tensor(act_lo[:, at], rx[:, i, :], act_hi[:, at].bitcast(F32), ALU.subtract).then_inc(tok_lo_ready, 1)
            logits, top, diff, ediff, first, second, chosen, weight, idx_f, tmp = rsm
            shape = [P, TT, E]
            dve.wait_ge(logits_ready, 1)
            own.link(dve.tensor_tensor(logits[:], ps[:, 6, 0:TT * E].rearrange("p (i e) -> p i e", e=E),
                                       b_router[:].unsqueeze(1).to_broadcast(shape), ALU.add))
            for i in range(TT):
                own.step(dve.max(top[:, i, :], logits[:, i, :]))
            own.settle()
            for i in range(TT):
                own.step(dve.max_index(ridx[:, i, :], top[:, i, :], logits[:, i, :]))
            dve.tensor_tensor(diff[:, :, 0:1], top[:, :, 1:2], top[:, :, 0:1], ALU.subtract).then_inc(top_ready, 1)
            own.settle()
            own.link(dve.tensor_copy(idx_f[:], ridx[:]))
            ids = expert_ids[:].unsqueeze(1).to_broadcast(shape)
            own.step(dve.tensor_tensor(first[:], ids, idx_f[:, :, 0:1].to_broadcast(shape), ALU.is_equal))
            own.link(dve.tensor_tensor(second[:], ids, idx_f[:, :, 1:2].to_broadcast(shape), ALU.is_equal))
            dve.tensor_tensor(chosen[:], first[:], second[:], ALU.add).then_inc(mask_ready, 1)
            dve.wait_ge(top_exp, 1)
            own.link(dve.tensor_scalar(weight[:, :, 0:1], ediff[:, :, 0:1], 1.0, None, ALU.add))
            own.link(dve.reciprocal(weight[:, :, 0:1], weight[:, :, 0:1]))
            own.link(dve.tensor_tensor(weight[:, :, 1:2], weight[:, :, 0:1], ediff[:, :, 0:1], ALU.mult))
            own.step(dve.tensor_tensor(first[:], first[:], weight[:, :, 0:1].to_broadcast(shape), ALU.mult))
            own.link(dve.tensor_tensor(second[:], second[:], weight[:, :, 1:2].to_broadcast(shape), ALU.mult))
            own.step(dve.tensor_tensor(gates[:], first[:], second[:], ALU.add))
            dve.wait_ge(ranks_ready, 1)
            own.link(dve.tensor_scalar(tmp[:], ps[:, 7, 0:TT * E].rearrange("p (i e) -> p i e", e=E), MISS, None, ALU.add))
            own.link(dve.tensor_tensor(tmp[:], tmp[:], chosen[:], ALU.mult))
            own.step(dve.tensor_scalar(rank[:], tmp[:], -MISS, None, ALU.add))
            own.settle()
            dve.wait_ge(tok_lo_ready, 2)
            dve.tensor_copy(counts[:], ps[:, 7, 2 * E:3 * E]).then_inc(routed, 1)

            def select(e, off):
                for i in range(TT):
                    dve.tensor_scalar(sel[:, i, :], slot_ids[:, off:off + P], rank[:, i, bass.ds(e, 1)], None,
                                      ALU.is_equal).then_inc(sel_ready, 1)

            def take_in(base):
                for b in range(2):
                    dve.wait_ge(in_hi_ready, base + (b + 1))
                    at = slice(b * BANK, (b + 1) * BANK)
                    dve.tensor_tensor(in_lo[:, at], ps[:, 2 + b, :], in_hi[:, at].bitcast(F32),
                                      ALU.subtract).then_inc(in_lo_ready, 1)

            def lo_of(u_base, u):
                dve.wait_ge(hi_ready, u_base + (N_PRE + u + 1))
                s = (N_PRE + u) % SPLIT_SLOTS
                dve.tensor_tensor(w_lo[s][:], raw[slot_of(N_PRE + u)][:], w_hi[s][:].bitcast(F32),
                                  ALU.subtract).then_inc(lo_ready, 1)

            def add_scattered(base):
                for i in range(TT):
                    for b in range(2):
                        dve.wait_ge(scattered, base + (2 * i + b + 1))
                        at = slice(b * BANK, (b + 1) * BANK)
                        dve.tensor_tensor(res[:, i, at], res[:, i, at], ps[:, 2 + 2 * i + b, :],
                                          ALU.add).then_inc(res_ready, 1)

            def one_pass(n, e, off, kind):
                u_base, t_base = held(dve, n * N_BODY), held(dve, n * MSTEPS)
                h_base, s_base = held(dve, n * 2), held(dve, n * 4)

                def mult(t):
                    dve.wait_ge(unit_used, u_base + (N_PRE + M_W3[t, 1] + 1))
                    dve.wait_ge(silu_ready, t_base + (t + 1))
                    dve.tensor_tensor(e_h[t % 2][:], e_h[t % 2][:], ps[:, 2 * (t % 2) + 1, :], ALU.mult).then_inc(h_ready, 1)

                def turned(t):
                    dve.wait_ge(hT_hi_ready, t_base + (t + 1))
                    dve.tensor_tensor(hT_lo[:], ps[:, 6, :], hT_hi[:].bitcast(F32), ALU.subtract).then_inc(hT_lo_ready, 1)

                if kind == "extra":
                    select(e, off)
                    lo_of(u_base, 0)
                    take_in(h_base)
                    lo_of(u_base, 1)
                    lo_of(u_base, 2)
                for u in range(3, N_BODY):
                    lo_of(u_base, u)
                    if u == M_W1[0, 1] + 3 and kind != "extra":
                        dve.wait_ge(res_ready, s_base + R_PRE)
                        add_scattered(s_base)
                    if u == M_W1[2, 1] + 3 and kind == "next":
                        dve.wait_ge(selT_turned, n + 1)
                        select(e + 1, 0)
                    for t in range(MSTEPS):
                        if t and u == M_W1[t, 1] + 3:
                            turned(t - 1)
                        if u == M_W3[t, 1] + 2:
                            mult(t)
                turned(MSTEPS - 1)
                if kind == "next":
                    take_in(h_base + 2)
                    for u in range(3):
                        lo_of(u_base, N_BODY + u)
                for b in range(2):
                    dve.wait_ge(out_hi_ready, h_base + (b + 1))
                    at = slice(b * BANK, (b + 1) * BANK)
                    dve.scalar_tensor_tensor(out=y_lo[:, at], in0=ps[:, 4 + b, :], scalar=slot_gate[:, 0:1],
                                             in1=y_hi[:, at].bitcast(F32), op0=ALU.mult,
                                             op1=ALU.subtract).then_inc(y_lo_split, 1)
                if kind != "next":
                    dve.wait_ge(res_ready, s_base + (R_PRE + 4))
                    add_scattered(s_base + 4)

            def first_tokens():
                dve.wait_ge(routed, 1)
                select(0, 0)
                dve.memset(y_lo[:].bitcast(F32), 0.0).then_inc(y_lo_split, 2)
                take_in(0)
                for u in range(3):
                    lo_of(0, u)

            experts(dve, lambda n, e, off: one_pass(n, e, off, "next"), first_tokens,
                    lambda n, e, off: one_pass(n, e, off, "last"), lambda n, e, off: one_pass(n, e, off, "extra"))


_INS = ["x", "positions", "norm_mix", "norm_ffn", "mla_w_in", "mla_g_qa", "mla_w_qb", "mla_g_kva", "mla_w_kvb",
        "mla_g_qn", "mla_g_kn", "mla_w_o", "lru_w_in", "lru_b_in", "lru_conv_w", "lru_conv_b", "lru_w_gate_a",
        "lru_b_gate_a", "lru_w_gate_i", "lru_b_gate_i", "lru_lambda", "lru_w_out", "lru_b_out", "ffn_w1",
        "ffn_w3", "ffn_w2", "moe_w_router", "moe_b_router", "moe_w1", "moe_w3", "moe_w2"]


def kernel(**inputs):
    import numpy as _np
    import concourse.bacc as _bacc
    from concourse import mybir as _mybir
    from concourse.bass_utils import run_bass_kernel_spmd as _run

    nc = _bacc.Bacc("TRN2", target_bir_lowering=False, num_devices=1)
    arrays = {f"in_{name}_dram": _np.ascontiguousarray(inputs[name]) for name in _INS}
    rope = inputs["mla_g_qn"].shape[1] - 128
    exponents = _np.arange(0, rope, 2, dtype=_np.float32) / _np.float32(rope)
    arrays["rope_freq_dram"] = (_np.float32(1.0) / _np.power(_np.float32(ROPE_BASE), exponents)).astype(_np.float32)
    args = [nc.dram_tensor(name, a.shape, _mybir.dt.from_np(a.dtype), kind="ExternalInput").ap()
            for name, a in arrays.items()]
    shape = inputs["x"].shape
    args.append(nc.dram_tensor("out_dram", shape, _mybir.dt.float32, kind="ExternalOutput").ap())
    encoder_trunk(nc, *args)
    return _run(nc, [arrays], core_ids=[0]).results[0]["out_dram"]
```

```python
from contextlib import ExitStack

import numpy as np

import concourse.bass as bass
from concourse import mybir

ALU = mybir.AluOpType
ACT = mybir.ActivationFunctionType
AX = mybir.AxisListType
F32 = mybir.dt.float32
F32R = mybir.dt.float32r
I32 = mybir.dt.int32
U32 = mybir.dt.uint32

P = 128
BANK = 512
SBUF_BASE, SBUF_END = 16512, 229344
NORM_EPS = 1e-6
ROPE_BASE = 10000.0
UNIT = 2048
RAW_SLOTS = 14
ATT_SLOTS = 5
SPLIT_SLOTS = 3
NEG = -1.0e30
MISS = 1000.0
TWO_PI_A = 6.28125
TWO_PI_B = round((2 * np.pi - TWO_PI_A) * 2 ** 21) / 2 ** 21
TWO_PI_C = float(2 * np.pi - TWO_PI_A - TWO_PI_B)
ROUND_MAGIC = 12582912.0
PI_FLOOR = 3.1415925


class Region:

    def __init__(self, nc, base, size):
        self.nc, self.base, self.at, self.end = nc, base, base, base + size

    def take(self, name, shape, dtype=F32):
        size = 4 * int(np.prod(shape[1:]))
        tensor = self.nc.alloc_sbuf_tensor_at(name, shape, dtype, offset=self.at)
        self.at += (size + 31) // 32 * 32
        assert self.at <= self.end, (name, self.at, self.end)
        return tensor

    def skip(self, size):
        part = Region(self.nc, self.at, size)
        self.at += size
        assert self.at <= self.end
        return part


class Chain:

    def __init__(self, engine, sem):
        self.engine, self.sem, self.count = engine, sem, 0

    def step(self, instruction):
        instruction.then_inc(self.sem, 1)
        self.count += 1

    def settle(self):
        self.engine.wait_ge(self.sem, self.count)

    def link(self, instruction):
        self.step(instruction)
        self.settle()


def encoder_trunk(nc, x, positions, norm_mix, norm_ffn, mla_w_in, mla_g_qa, mla_w_qb, mla_g_kva,
                  mla_w_kvb, mla_g_qn, mla_g_kn, mla_w_o, lru_w_in, lru_b_in, lru_conv_w,
                  lru_conv_b, lru_w_gate_a, lru_b_gate_a, lru_w_gate_i, lru_b_gate_i, lru_lambda,
                  lru_w_out, lru_b_out, ffn_w1, ffn_w3, ffn_w2, moe_w_router, moe_b_router,
                  moe_w1, moe_w3, moe_w2, inv_freq, out):
    _, SEQ, D = x.shape
    TT = SEQ // P
    KD = D // P
    Q_LORA, KV_LORA = mla_g_qa.shape[1], mla_g_kva.shape[1]
    QK_HEAD = mla_g_qn.shape[1]
    HEADS = mla_w_qb.shape[2] // QK_HEAD
    V_HEAD = mla_w_o.shape[1] // HEADS
    NOPE = mla_w_kvb.shape[2] // HEADS - V_HEAD
    ROPE = QK_HEAD - NOPE
    HALF = ROPE // 2
    CAT = mla_w_in.shape[2]
    LAT = (Q_LORA + KV_LORA) // P
    KQ, KKV = Q_LORA // P, KV_LORA // P
    FF = ffn_w1.shape[2]
    LRU_HEADS, E = lru_w_gate_a.shape[1], moe_w1.shape[1]
    EFF = moe_w1.shape[3]
    assert (TT, KD, HEADS, NOPE, ROPE, V_HEAD, E, LRU_HEADS) == (2, 8, 8, 128, 64, 128, 8, 8)

    def rows_of(w, c0, n, cols=slice(None)):
        return w[c0 * P:(c0 + n) * P, cols].rearrange("(k p) n -> p k n", p=P)

    units = []

    def add(*parts):
        units.append(parts)
        return len(units) - 1

    w_in, w_qb, w_kvb, w_o = mla_w_in[0], mla_w_qb[0], mla_w_kvb[0], mla_w_o[0]
    U_WIN = [add((0, rows_of(w_in, 2 * i, 2))) for i in range(KD // 2)]
    U_KV = [add((0, rows_of(w_kvb, 0, KKV, slice(i * 1024, (i + 1) * 1024)))) for i in range(2)]
    U_Q = [add((0, rows_of(w_qb, 0, KQ, slice(i * BANK, (i + 1) * BANK)))) for i in range(3)]
    U_WO = [add((0, rows_of(w_o, 2 * i, 2))) for i in range(4)]
    N_ATT = len(units)
    FSTEPS = FF // 256
    assert FF == 256 * FSTEPS
    U_F1, U_F3, U_F2 = {}, {}, {}
    for s in range(FSTEPS + 1):
        cols = slice(s * 256, (s + 1) * 256)
        if s < FSTEPS:
            U_F1[s] = add((0, rows_of(ffn_w1[0], 0, KD, cols)))
        if s:
            U_F2[s - 1] = add((0, rows_of(ffn_w2[0], 2 * (s - 1), 2)))
        if s < FSTEPS:
            U_F3[s] = add((0, rows_of(ffn_w3[0], 0, KD, cols)))
    LSTEPS = LRU_HEADS // 2
    lru_steps = [("X", 0)]
    for s in range(LSTEPS):
        lru_steps.append(("G", s))
        if s + 1 < LSTEPS:
            lru_steps.append(("X", s + 1))
            if s:
                lru_steps.append(("O", s - 1))
        lru_steps.append(("GA", s))
    lru_steps += [("O", LSTEPS - 2), ("O", LSTEPS - 1)]
    U_X, U_G, U_GA, U_O = {}, {}, {}, {}
    for kind, s in lru_steps:
        if kind == "X":
            U_X[s] = add((0, rows_of(lru_w_in[0], 0, KD, slice(D + s * 256, D + (s + 1) * 256))))
        elif kind == "G":
            U_G[s] = add((0, rows_of(lru_w_in[0], 0, KD, slice(s * 256, (s + 1) * 256))))
        elif kind == "O":
            U_O[s] = add((0, rows_of(lru_w_out[0], 2 * s, 2)))
        else:
            U_GA[s] = add((0, lru_w_gate_a[0, 2 * s:2 * s + 2].rearrange("h i j -> i h j")),
                          (256, lru_w_gate_i[0, 2 * s:2 * s + 2].rearrange("h i j -> i h j")))
    N_PRE = len(units)
    width = [max(c + p.shape[1] * p.shape[2] for c, p in u) for u in units]

    MSTEPS = EFF // BANK
    assert EFF == MSTEPS * BANK
    M_W1, M_W3, M_W2 = {}, {}, {}
    body_units = []
    for t in range(MSTEPS + 1):
        if t < MSTEPS:
            for name, table in (("w1", M_W1), ("w3", M_W3)):
                for half in range(2):
                    table[t, half] = len(body_units)
                    body_units.append((name, t, half))
        if t:
            for half in range(2):
                M_W2[t - 1, half] = len(body_units)
                body_units.append(("w2", t - 1, half))
    N_BODY = len(body_units)
    assert N_BODY % RAW_SLOTS == 0 and N_BODY % SPLIT_SLOTS == 0
    OCC = N_BODY // RAW_SLOTS

    order = [(N_ATT + i) % ATT_SLOTS for i in range(ATT_SLOTS)] + list(range(ATT_SLOTS, RAW_SLOTS))

    def slot_of(g):
        return g % ATT_SLOTS if g < N_ATT else order[(g - N_ATT) % RAW_SLOTS]

    landed_at, count = [], [0] * RAW_SLOTS
    for g, parts in enumerate(units):
        count[slot_of(g)] += 16 * len(parts)
        landed_at.append(count[slot_of(g)])
    for g in range(N_PRE, N_PRE + SPLIT_SLOTS):
        landed_at.append(count[slot_of(g)] + 16)
        width.append(UNIT)
    slot_count = list(count)

    sbuf = Region(nc, SBUF_BASE, SBUF_END - SBUF_BASE)
    res = sbuf.take("residual", [P, TT, D])
    act_hi = sbuf.take("act_hi", [P, KD * SEQ], F32R)
    act_lo = sbuf.take("act_lo", [P, KD * SEQ], F32R)
    mid = sbuf.skip(18432)
    raw_region = sbuf.skip(RAW_SLOTS * UNIT * 4)
    w_hi = [sbuf.take(f"w_hi{i}", [P, UNIT], F32R) for i in range(SPLIT_SLOTS)]
    w_lo = [sbuf.take(f"w_lo{i}", [P, UNIT], F32R) for i in range(SPLIT_SLOTS)]
    raw = [Region(nc, raw_region.base + i * UNIT * 4, UNIT * 4).take(f"w_raw{i}", [P, UNIT])
           for i in range(RAW_SLOTS)]
    ident = sbuf.take("ident", [P, P])
    rows = sbuf.take("vector_rows", [P, P])
    lam = [sbuf.take(f"lam{i}", [P, LRU_HEADS]) for i in range(6)]
    cols = sbuf.take("vector_cols", [P, P])
    ones = sbuf.take("ones", [P, P])
    before = sbuf.take("before", [P, P])
    slot_ids = sbuf.take("slot_ids", [P, 2 * P])
    expert_ids = sbuf.take("expert_ids", [P, E])
    w_router = sbuf.take("w_router", [P, KD, E])
    b_router = sbuf.take("b_router", [P, E])
    sumsq = sbuf.take("sumsq", [P, 8])
    rstd = sbuf.take("rstd", [P, 8])
    minus_half = sbuf.take("minus_half", [P, 16])
    rank = sbuf.take("rank", [P, TT, E])
    gates = sbuf.take("gates", [P, TT, E])
    counts = sbuf.take("counts", [P, E], I32)
    slot_gate = sbuf.take("slot_gate", [P, 1])
    decay = sbuf.take("decay", [P, 2, LRU_HEADS])

    def over(base, size):
        return Region(nc, base, size)

    m = over(mid.base, 18432)
    trig = [m.take(f"trig{i}", [P, TT, HALF]) for i in range(4)]
    m = over(mid.base + 8192, 18432 - 8192)
    xn = m.take("x_normed", [P, TT, D])
    m = over(mid.base, 18432)
    kr = m.take("k_rope", [P, TT, HEADS, ROPE])
    qr = m.take("q_rope", [P, TT, HEADS, ROPE])
    rope_t = [m.take(f"rope_t{i}", [P, TT, HEADS, HALF]) for i in range(4)]
    junk = over(mid.base + 8192, 8192).take("squares", [P, UNIT])
    m = over(mid.base, 18432)
    f_h = [m.take(f"ffn_h{i}", [P, BANK]) for i in range(2)]
    f_hi = m.take("ffn_h_hi", [P, BANK], F32R)
    f_lo = m.take("ffn_h_lo", [P, BANK], F32R)
    m = over(mid.base, 18432)
    xpad = m.take("xb_padded", [P, 2, SEQ + 4])
    xc = m.take("xb_conv", [P, 2, SEQ])
    lc_hi = m.take("lru_hi", [P, 2, SEQ], F32R)
    lc_lo_at = m.at
    lc_lo = m.take("lru_lo", [P, 2, SEQ], F32R)
    gate = m.take("gate", [P, 2, SEQ])
    ra_at = m.at
    ra = m.take("r_then_a", [P, 2, SEQ])
    iu = m.take("i_then_y", [P, 2, SEQ])
    tm_at = m.at
    tm = m.take("t_then_mult", [P, 2, SEQ])
    a_squared = over(lc_lo_at, 2048).take("a_squared", [P, 2, SEQ])
    m = over(ra_at, 2048)
    ly_hi = m.take("lru_y_hi", [P, 2, SEQ], F32R)
    m = over(tm_at, 2048)
    ly_lo = m.take("lru_y_lo", [P, 2, SEQ], F32R)
    m = over(mid.base, 18432)
    rx = m.take("router_x", [P, TT, D])
    rxT = m.take("router_xT", [P, KD, SEQ])
    rsm = [m.take(f"router_small{i}", [P, TT, 8]) for i in range(10)]
    ridx = m.take("router_idx", [P, TT, 8], U32)
    m = over(mid.base, 18432)
    in_hi = m.take("expert_in_hi", [P, D], F32R)
    in_lo = m.take("expert_in_lo", [P, D], F32R)
    y_at = m.at
    e_h = [m.take(f"expert_h{i}", [P, BANK]) for i in range(2)]
    hT_hi = m.take("expert_hT_hi", [P, BANK], F32R)
    hT_lo = m.take("expert_hT_lo", [P, BANK], F32R)
    y_m = over(y_at, 8192)
    y_hi = y_m.take("expert_out_hi", [P, D], F32R)
    y_lo = y_m.take("expert_out_lo", [P, D], F32R)
    sel = m.take("select", [P, TT, P], F32R)
    selT = m.take("select_T", [P, SEQ], F32R)

    far = over(raw_region.base + ATT_SLOTS * UNIT * 4, (RAW_SLOTS - ATT_SLOTS) * UNIT * 4)
    hcat_at = far.at
    hcat = far.take("hcat", [P, TT, CAT])
    lat_at = far.at
    lat_hi = far.take("latent_hi", [P, LAT, SEQ], F32R)
    lat_lo = far.take("latent_lo", [P, LAT, SEQ], F32R)
    qn = far.take("q", [P, TT, HEADS, QK_HEAD])
    kn = far.take("k_nope", [P, TT, HEADS, NOPE])
    vt = far.take("v", [P, TT, HEADS, V_HEAD])
    qT_at = far.at
    qT = far.take("qT_nope", [P, HEADS, SEQ])
    act_junk = over(qT_at, 8192).take("act_squares", [P, UNIT])
    qrT = far.take("qT_rope", [P, HEADS, SEQ])
    kT = far.take("kT_nope", [P, HEADS, SEQ])
    mask = far.take("mask", [P, P])
    g_rope = far.take("g_rope", [P, 2 * ROPE])
    pos_i = far.take("pos_i", [P, TT], I32)
    freq = far.take("freq", [P, HALF])
    cos = far.take("cos", [P, TT, HALF])
    sin = far.take("sin", [P, TT, HALF])
    ssh = far.take("head_sumsq", [P, 2, TT * HEADS])
    rsh = far.take("head_rstd", [P, 2, TT * HEADS])
    ssr = far.take("rope_sumsq", [P, TT])
    krT = over(hcat_at, 5632).take("kT_rope", [P, HEADS // 2, SEQ])
    q_junk = over(lat_at, 6144).take("q_squares", [P, HEADS * QK_HEAD])
    soft = over(lat_at, 10240)
    pr = [soft.take(f"probs{i}", [P, 3 * P]) for i in range(4)]
    prT = [soft.take(f"probs_T{i}", [P, 3 * P]) for i in range(2)]
    smax = soft.take("smax", [P, HEADS, 2])
    ssum = soft.take("ssum", [P, HEADS, 2])
    sinv = soft.take("sinv", [P, HEADS, 2])

    R_MIX, R_FFN, R_QA, R_KVA, R_QN, R_KN, R_BIN, R_CW, R_CB, R_BA, R_BI, R_LAM, R_BO, R_GR = (
        0, 16, 32, 35, 37, 38, 39, 55, 87, 95, 103, 111, 119, 127)
    vectors = [
        (R_MIX, norm_mix.rearrange("l (k p) -> (l k) p", p=P)),
        (R_FFN, norm_ffn.rearrange("l (k p) -> (l k) p", p=P)),
        (R_QA, mla_g_qa.rearrange("l (k p) -> (l k) p", p=P)),
        (R_KVA, mla_g_kva.rearrange("l (k p) -> (l k) p", p=P)),
        (R_QN, mla_g_qn[:, 0:NOPE]), (R_KN, mla_g_kn[:, 0:NOPE]),
        (R_BIN, lru_b_in.rearrange("l (k p) -> (l k) p", p=P)),
        (R_CW, lru_conv_w[0].rearrange("j (k p) -> (j k) p", p=P)),
        (R_CB, lru_conv_b.rearrange("l (k p) -> (l k) p", p=P)),
        (R_BA, lru_b_gate_a[0]), (R_BI, lru_b_gate_i[0]),
        (R_LAM, lru_lambda.rearrange("l (k p) -> (l k) p", p=P)),
        (R_BO, lru_b_out.rearrange("l (k p) -> (l k) p", p=P)),
    ]

    ctx = ExitStack()
    with ctx:
        ps = ctx.enter_context(nc.psum_tensor("ps", [P, 8, BANK], F32))

        def sem(name):
            return ctx.enter_context(nc.semaphore(name))

        raw_landed = [sem(f"raw_landed{i}") for i in range(RAW_SLOTS)]
        hi_ready = sem("hi_ready")
        lo_ready = sem("lo_ready")
        unit_used = sem("unit_used")
        trig_ready = sem("trig_ready")
        mix_landed = sem("mix_landed")
        x_landed, vec_landed, small_landed, pos_landed = (
            sem("x_landed"), sem("vec_landed"), sem("small_landed"), sem("pos_landed"))
        const_ready = sem("const_ready")
        rows_turned = sem("rows_turned")
        cols_ready = sem("cols_ready")
        sq_act, sq_dve = sem("sq_act"), sem("sq_dve")
        rstd_ready = sem("rstd_ready")
        xn0_ready, xn_ready = sem("xn0_ready"), sem("xn_ready")
        xn_turned = sem("xn_turned")
        act_hi_ready, act_lo_ready = sem("act_hi_ready"), sem("act_lo_ready")
        sum_ready = sem("sum_ready")
        res_ready = sem("res_ready")
        cat_ready = sem("cat_ready")
        cat_sq = sem("cat_sq")
        lat_rstd, lat_turned = sem("lat_rstd"), sem("lat_turned")
        lat_hi_ready, lat_lo_ready = sem("lat_hi_ready"), sem("lat_lo_ready")
        kv0_copied, kv1_copied, q_copied = sem("kv0_copied"), sem("kv1_copied"), sem("q_copied")
        kn0_scaled = sem("kn0_scaled")
        head_sq, head_sq_act, head_rstd = sem("head_sq"), sem("head_sq_act"), sem("head_rstd")
        kq_normed, kq_turned = sem("kq_normed"), sem("kq_turned")
        kqT_act, kqT_dve = sem("kqT_act"), sem("kqT_dve")
        scores_ready, smax_ready, exp_ready = sem("scores_ready"), sem("smax_ready"), sem("exp_ready")
        probs_ready, probs_turned, probsT_ready = (
            sem("probs_ready"), sem("probs_turned"), sem("probsT_ready"))
        pv_ready, o_hi_ready, o_lo_ready = sem("pv_ready"), sem("o_hi_ready"), sem("o_lo_ready")
        f_silu, f_h_ready, f_hi_ready, f_lo_ready = (
            sem("f_silu"), sem("f_h_ready"), sem("f_hi_ready"), sem("f_lo_ready"))
        xb_ready, conv_ready, xc_hi_ready, xc_lo_ready = (
            sem("xb_ready"), sem("conv_ready"), sem("xc_hi_ready"), sem("xc_lo_ready"))
        gate_ready, sig_ready, at_ready, v_ready, mult_ready = (
            sem("gate_ready"), sem("sig_ready"), sem("at_ready"), sem("v_ready"), sem("mult_ready"))
        y_ready, y_hi_ready, y_lo_ready = sem("y_ready"), sem("y_hi_ready"), sem("y_lo_ready")
        lam_exp, lam_ready = sem("lam_exp"), sem("lam_ready")
        w_gained = sem("w_gained")
        gain_rows, rx_ready, rx_turned, rxT_ready = (
            sem("gain_rows"), sem("rx_ready"), sem("rx_turned"), sem("rxT_ready"))
        tok_hi_ready, tok_lo_ready = sem("tok_hi_ready"), sem("tok_lo_ready")
        logits_ready, top_ready, top_exp, mask_ready, ranks_ready, routed = (
            sem("logits_ready"), sem("top_ready"), sem("top_exp"), sem("mask_ready"),
            sem("ranks_ready"), sem("routed"))
        sel_ready, gathered, selT_turned = sem("sel_ready"), sem("gathered"), sem("selT_turned")
        in_hi_ready, in_lo_ready = sem("in_hi_ready"), sem("in_lo_ready")
        y_lo_split, y_zeroed = sem("y_lo_split"), sem("y_zeroed")
        selT_ready, gate_col_ready = sem("selT_ready"), sem("gate_col_ready")
        silu_ready, h_ready = sem("silu_ready"), sem("h_ready")
        h_turned, hT_hi_ready, hT_lo_ready = sem("h_turned"), sem("hT_hi_ready"), sem("hT_lo_ready")
        out_hi_ready = sem("out_hi_ready")
        scattered = sem("scattered")
        dve_own, pool_own, out_sem = sem("dve_own"), sem("pool_own"), sem("out_sem")

        R_PRE = 3 * 2 * TT

        block = ctx.enter_context(nc.Block())

        def experts(engine, body, prologue=None, last=None, extra=None):
            if prologue:
                prologue()
            with engine.Fori(0, E - 1 if last else E) as e:
                body(e, e, 0)
            if last:
                last(E - 1, E - 1, 0)
            engine.wait_ge(routed, 1)
            done = engine.alloc_register(f"passes_{engine.engine.name}")
            engine.reg_mov(done, E)
            with engine.Fori(0, E) as e:
                n_tokens = engine.value_load(counts[0:1, bass.ds(e, 1)], min_val=0, max_val=SEQ)
                with engine.If(n_tokens > P):
                    (extra or body)(engine.snap(done, min_val=E, max_val=2 * E), e, P)
                    engine.reg_add(done, done, 1)
            return engine.snap(done, min_val=E, max_val=2 * E)

        def held(engine, value):
            return value if isinstance(value, int) else engine.snap(value)

        def y_parts(s):
            if s < LSTEPS - 2:
                return ly_hi[:], ly_lo[:]
            at = (s - LSTEPS + 2) * 2 * SEQ
            return tuple(t[:, at:at + 2 * SEQ].rearrange("p (c t) -> p c t", c=2) for t in (act_hi, act_lo))

        def lru_order(split, x_work, g_work, a_work):
            split(U_X[0] + 2)
            for i, (kind, s) in enumerate(lru_steps[:-2]):
                g = U_X[0] + i
                if kind == "GA":
                    a_work(s)
                else:
                    split(g + SPLIT_SLOTS)
                if kind == "X":
                    x_work(s)
                elif kind == "G" and g_work:
                    g_work(s)
            split(N_PRE + 1)

        @block.sync
        def _(sp):
            sp.dma_start(rows[0:R_FFN, :], vectors[0][1]).then_inc(mix_landed, 16)
            for i in range(TT):
                sp.dma_start(res[:, i, :], x[0, i * P:(i + 1) * P, :]).then_inc(x_landed, 16)
            for g, parts in enumerate(units):
                if g < N_ATT:
                    if g >= ATT_SLOTS:
                        sp.wait_ge(lo_ready, g - ATT_SLOTS + 1)
                elif g < N_ATT + ATT_SLOTS:
                    sp.wait_ge(lo_ready, g - ATT_SLOTS + 1)
                elif g < N_ATT + RAW_SLOTS:
                    sp.wait_ge(pv_ready, HEADS)
                else:
                    sp.wait_ge(lo_ready, g - RAW_SLOTS + 1)
                for c0, src in parts:
                    n, w = src.shape[1], src.shape[2]
                    dst = raw[slot_of(g)][:, c0:c0 + n * w].rearrange("p (k n) -> p k n", k=n)
                    sp.dma_start(dst, src).then_inc(raw_landed[slot_of(g)], 16)

            def body(n, e, off):
                base = sp.snap(n * N_BODY)
                w1, w3, w2 = (w[0, bass.ds(e, 1)] for w in (moe_w1, moe_w3, moe_w2))
                for u, (name, t, half) in enumerate(body_units):
                    if name == "w2":
                        r0 = t * BANK + half * 256
                        src = w2[:, r0:r0 + 256, :].rearrange("o (k p) n -> p (o k) n", p=P)
                    else:
                        w = w1 if name == "w1" else w3
                        src = w[:, half * 512:half * 512 + 512, t * BANK:(t + 1) * BANK]
                        src = src.rearrange("o (k p) n -> p (o k) n", p=P)
                    slot = slot_of(N_PRE + u)
                    dst = raw[slot][:, :].rearrange("p (k n) -> p k n", k=src.shape[1])
                    sp.wait_ge(lo_ready, base + (N_PRE + u - RAW_SLOTS + 1))
                    sp.dma_start(dst, src).then_inc(raw_landed[slot], 16)

            done = experts(sp, body)
            for i in range(TT):
                sp.wait_ge(res_ready, sp.snap(done * 4 + (R_PRE + 2 * (i + 1))))
                sp.dma_start(out[0, i * P:(i + 1) * P, :], res[:, i, :]).then_inc(out_sem, 16)
            sp.wait_ge(out_sem, 16 * TT)

        @block.gpsimd
        def _(pool):
            own = Chain(pool, pool_own)

            def power(dst, src, n, scale, bias, done):
                own.link(pool.tensor_scalar(dst, src, scale, bias, ALU.mult, ALU.add))
                pool.tensor_tensor(dst, dst, minus_half[:, 0:n], ALU.pow).then_inc(done, 1)

            def norm(i):
                pool.wait_ge(sq_act, i + 1)
                pool.wait_ge(sq_dve, i + 1)
                power(rstd[:, 0:2], sumsq[:, 0:2], 2, 1.0 / D, NORM_EPS, rstd_ready)

            own.step(pool.memset(ident[:], 0.0))
            own.settle()
            pool.affine_select(out=ident[:], in_=ident[:], compare_op=ALU.not_equal, fill=1.0,
                               base=0, pattern=[[-1, P]], channel_multiplier=1).then_inc(const_ready, 1)
            for r, src in vectors[1:]:
                pool.dma_start(rows[r:r + src.shape[0], :], src).then_inc(vec_landed, 16)
            pool.dma_start(rows[R_GR:R_GR + 1, 0:ROPE], mla_g_qn[:, NOPE:QK_HEAD]).then_inc(vec_landed, 16)
            pool.dma_start(rows[R_GR:R_GR + 1, ROPE:2 * ROPE], mla_g_kn[:, NOPE:QK_HEAD]).then_inc(vec_landed, 16)
            with nc.allow_non_contiguous_dma(reason="256 positions, one per token"):
                pool.dma_start(pos_i[:], positions[0].rearrange("(i p) -> p i", p=P)).then_inc(pos_landed, 16)
            pool.dma_start(freq[:], inv_freq.partition_broadcast(P)).then_inc(pos_landed, 16)
            pool.dma_start(w_router[:], moe_w_router[0].rearrange("(k p) e -> p k e", p=P)).then_inc(small_landed, 16)
            pool.dma_start(b_router[:], moe_b_router[0].partition_broadcast(P)).then_inc(small_landed, 16)
            own.step(pool.memset(before[:], 1.0))
            own.step(pool.memset(mask[:], 0.0))
            own.settle()
            own.step(pool.memset(minus_half[:], -0.5))
            own.settle()
            norm(0)
            own.step(pool.memset(ones[:], 1.0))
            own.step(pool.affine_select(out=before[:], in_=before[:], compare_op=ALU.is_gt, fill=0.0,
                                        base=0, pattern=[[1, P]], channel_multiplier=-1))
            own.step(pool.memset(mask[0:P // 2, P // 2:P], NEG))
            own.step(pool.iota(slot_ids[:], pattern=[[1, 2 * P]], base=0, channel_multiplier=0,
                               allow_small_or_imprecise_dtypes=True))
            own.step(pool.iota(expert_ids[:], pattern=[[1, E]], base=0, channel_multiplier=0,
                               allow_small_or_imprecise_dtypes=True))
            own.step(pool.memset(qrT[:], 0.0))
            own.settle()
            pool.memset(sumsq[:, 7:8], 0.0).then_inc(const_ready, 1)

            pool.wait_ge(cat_sq, 4)
            own.link(pool.tensor_scalar(rstd[:, 2:4], sumsq[:, 2:4], 1.0 / Q_LORA, NORM_EPS, ALU.mult, ALU.add))
            own.link(pool.tensor_scalar(rstd[:, 4:6], sumsq[:, 4:6], 1.0 / KV_LORA, NORM_EPS, ALU.mult, ALU.add))
            pool.tensor_tensor(rstd[:, 2:6], rstd[:, 2:6], minus_half[:, 0:4], ALU.pow).then_inc(lat_rstd, 1)
            pool.wait_ge(head_sq_act, 8)
            pool.wait_ge(head_sq, TT + 8)
            for i in range(TT):
                own.step(pool.tensor_scalar(ssh[:, 0, i * HEADS:(i + 1) * HEADS], ssh[:, 0, i * HEADS:(i + 1) * HEADS],
                                            ssr[:, i:i + 1], None, ALU.add))
            own.settle()
            power(rsh[:, 0, :], ssh[:, 0, :], 16, 1.0 / QK_HEAD, NORM_EPS, head_rstd)
            pool.wait_ge(head_sq_act, 16)
            pool.wait_ge(head_sq, TT + 16)
            power(rsh[:, 1, :], ssh[:, 1, :], 16, 1.0, QK_HEAD * NORM_EPS, head_rstd)
            for i in range(1, 4):
                norm(i)
            pool.wait_ge(routed, 1)
            pool.memset(y_hi[:].bitcast(F32), 0.0).then_inc(y_zeroed, 1)

        def split_ap(g):
            return w_hi[g % SPLIT_SLOTS], w_lo[g % SPLIT_SLOTS]

        @block.tensor
        def _(pe):
            def product(dst, a, b, start, stop):
                pe.matmul(dst, a[0], b[0], start=start, stop=False)
                pe.matmul(dst, a[0], b[1], start=False, stop=False)
                return pe.matmul(dst, a[1], b[0], start=False, stop=stop)

            def parts(pair, *index):
                return tuple(t[index] for t in pair)

            acts = (act_hi, act_lo)

            def token_block(k, i):
                return tuple(t[:, k * SEQ + i * P:k * SEQ + (i + 1) * P] for t in acts)

            def tokens(k):
                return tuple(t[:, k * SEQ:(k + 1) * SEQ] for t in acts)

            def cols_of(g, c0, n):
                return tuple(t[:, c0:c0 + n] for t in split_ap(g))

            def use(g):
                pe.wait_ge(lo_ready, g + 1)

            pe.wait_ge(const_ready, 1)
            pe.wait_ge(mix_landed, 16)
            pe.transpose(ps[:, 0, 0:R_FFN], rows[0:R_FFN, :], ident[0:R_FFN, 0:R_FFN]).then_inc(rows_turned, 1)

            def turn_norm(i):
                src = xn if i else res
                if i:
                    pe.wait_ge(xn0_ready, i)
                    pe.wait_ge(xn_ready, i)
                else:
                    pe.wait_ge(x_landed, 16 * TT)
                for b in range(KD // 2):
                    for kk in range(2):
                        for t in range(TT):
                            ins = pe.transpose(ps[:, 4 + b, kk * SEQ + t * P:kk * SEQ + (t + 1) * P],
                                               src[:, t, (2 * b + kk) * P:(2 * b + kk + 1) * P], ident[:])
                    ins.then_inc(xn_turned, 1)

            turn_norm(0)
            pe.wait_ge(cols_ready, 1)
            for j, g in enumerate(U_WIN):
                use(g)
                for kk in range(2):
                    k = 2 * j + kk
                    pe.wait_ge(act_lo_ready, k + 1)
                    for i in range(TT):
                        for c in range(2):
                            w = CAT // 2
                            ins = product(ps[:, 2 * i + c, 0:w], token_block(k, i),
                                          cols_of(g, kk * CAT + c * w, w), k == 0, k == KD - 1)
                ins.then_inc(unit_used, 1)
            pe.wait_ge(vec_landed, 16 * (len(vectors) + 1))
            pe.transpose(ps[:, 7, 0:P], rows[:], ident[:])
            pe.matmul(ps[:, 7, P:2 * P], ident[:, R_GR:R_GR + 1].to_broadcast([P, P]), rows[:],
                      start=True, stop=True).then_inc(rows_turned, 1)
            pe.wait_ge(cat_ready, 2 * TT)
            for c in range(LAT):
                for i in range(TT):
                    ins = pe.transpose(ps[:, 4 + c // 2, c % 2 * SEQ + i * P:c % 2 * SEQ + (i + 1) * P],
                                       hcat[:, i, c * P:(c + 1) * P], ident[:])
                ins.then_inc(lat_turned, 1)
            lat = (lat_hi, lat_lo)
            for j, g in enumerate(U_KV):
                use(g)
                pe.wait_ge(lat_lo_ready, LAT)
                pe.wait_ge(cols_ready, 2)
                for i in range(TT):
                    for c in range(2):
                        for k in range(KKV):
                            ins = product(ps[:, 4 * j + 2 * i + c, :],
                                          parts(lat, slice(None), KQ + k, slice(i * P, (i + 1) * P)),
                                          cols_of(g, k * 1024 + c * BANK, BANK), k == 0, k == KKV - 1)
                ins.then_inc(unit_used, 1)
            for j, g in enumerate(U_Q):
                use(g)
                for i in range(TT):
                    pe.wait_ge(kv1_copied if j == 1 else kv0_copied, 2 * i + (6 if j == 2 else 2))
                    for k in range(KQ):
                        ins = product(ps[:, 2 * j + i, :],
                                      parts(lat, slice(None), k, slice(i * P, (i + 1) * P)),
                                      cols_of(g, k * BANK, BANK), k == 0, k == KQ - 1)
                ins.then_inc(unit_used, 1)
            pe.wait_ge(kv0_copied, 8)
            pe.wait_ge(kv1_copied, 8)
            pe.wait_ge(q_copied, 6)
            for b in range(12):
                bank = (6 + b) % 8
                if b == 4:
                    pe.wait_ge(kn0_scaled, HEADS)
                    pe.wait_ge(kq_normed, 1)
                elif b >= 8:
                    pe.wait_ge(kq_normed, 3 if b < 10 else 5)
                    pe.wait_ge(kqT_act, b // 2 - 3)
                    pe.wait_ge(kqT_dve, b // 2 - 3)
                for kk in range(2):
                    for i in range(TT):
                        if b < 4:
                            src = qn[:, i, 2 * b + kk, 0:NOPE]
                        elif b < 8:
                            src = kn[:, i, 2 * (b - 4) + kk, :]
                        elif b < 10:
                            p = 2 * (b - 8) + kk
                            src = kr[:, i, 2 * p:2 * p + 2, :].rearrange("p h d -> p (h d)")
                        else:
                            p = 2 * (b - 10) + kk
                            src = qr[:, i, 2 * p:2 * p + 2, :].rearrange("p h d -> p (h d)")
                        ins = pe.transpose(ps[:, bank, kk * SEQ + i * P:kk * SEQ + (i + 1) * P], src, ident[:])
                ins.then_inc(kq_turned, 1)
            pe.wait_ge(kqT_act, 7)
            pe.wait_ge(kqT_dve, 7)

            def scores(h):
                if h >= 4:
                    pe.wait_ge(exp_ready, 2 * (h - 3))
                for i in range(TT):
                    dst = ps[:, h % 4, i * P:i * P + (i + 1) * P]
                    pe.matmul(dst, qT[:, h, i * P:(i + 1) * P], kT[:, h, 0:(i + 1) * P],
                              start=True, stop=False)
                    pe.matmul(dst, qrT[:, h, i * P:(i + 1) * P], krT[:, h // 2, 0:(i + 1) * P],
                              start=False, stop=False)
                    ins = pe.matmul(ps[:, h % 4, 2 * i * P:(2 * i + 1) * P], ident[:], mask[:],
                                    start=False, stop=True)
                ins.then_inc(scores_ready, 1)

            def turn_probs(h):
                pe.wait_ge(probs_ready, 2 * (h + 1))
                if h >= 2:
                    pe.wait_ge(probsT_ready, h - 1)
                for j in range(3):
                    ins = pe.transpose(ps[:, 4 + h % 2, j * P:(j + 1) * P], pr[h % 4][:, j * P:(j + 1) * P],
                                       ident[:])
                ins.then_inc(probs_turned, 1)

            def values(h):
                pe.wait_ge(probsT_ready, h + 1)
                if h >= 2:
                    pe.wait_ge(o_lo_ready, h - 1)
                pe.matmul(ps[:, 6 + h % 2, 0:SEQ], vt[:, 0, h, :], prT[h % 2][:, 0:SEQ],
                          start=True, stop=False)
                pe.matmul(ps[:, 6 + h % 2, P:SEQ], vt[:, 1, h, :], prT[h % 2][:, SEQ:3 * P],
                          start=False, stop=True).then_inc(pv_ready, 1)

            for h in range(HEADS + 3):
                if h < HEADS:
                    scores(h)
                if 2 <= h < HEADS + 2:
                    turn_probs(h - 2)
                if h >= 3:
                    values(h - 3)

            def into_residual(g, chunk_parts, first, last):
                use(g)
                if last:
                    for i in range(TT):
                        for c in range(2):
                            for kk in range(2):
                                ins = product(ps[:, 2 * i + c, :], chunk_parts(kk, i),
                                              cols_of(g, kk * D + c * BANK, BANK), first and kk == 0, kk == 1)
                            ins.then_inc(unit_used if (i, c) == (TT - 1, 1) else sum_ready, 1)
                    return
                for kk in range(2):
                    for i in range(TT):
                        a = chunk_parts(kk, i)
                        for c in range(2):
                            ins = product(ps[:, 2 * i + c, :], a, cols_of(g, kk * D + c * BANK, BANK),
                                          first and kk == 0, False)
                ins.then_inc(unit_used, 1)

            for j, g in enumerate(U_WO):
                pe.wait_ge(o_lo_ready, 2 * j + 2)
                into_residual(g, lambda kk, i: token_block(2 * j + kk, i), j == 0, j == 3)

            turn_norm(1)

            def ffn_up(g, s, which):
                use(g)
                for c in range(2):
                    for k in range(KD):
                        if s == 0 and which == 0 and c == 0:
                            pe.wait_ge(act_lo_ready, KD + k + 1)
                        ins = product(ps[:, 4 + 2 * (s % 2) + which, c * SEQ:(c + 1) * SEQ],
                                      cols_of(g, k * 256 + c * P, P), tokens(k), k == 0, k == KD - 1)
                ins.then_inc(unit_used, 1)

            def ffn_down(s):
                pe.wait_ge(f_lo_ready, s + 1)
                if s == 0:
                    pe.wait_ge(res_ready, 4)
                into_residual(U_F2[s], lambda kk, i: (f_hi[:, kk * SEQ + i * P:kk * SEQ + (i + 1) * P],
                                                      f_lo[:, kk * SEQ + i * P:kk * SEQ + (i + 1) * P]),
                              s == 0, s == FSTEPS - 1)

            for s in range(FSTEPS + 1):
                if s < FSTEPS:
                    if s == 0:
                        pe.wait_ge(act_lo_ready, KD + 2)
                    if s >= 2:
                        pe.wait_ge(f_h_ready, s - 1)
                    ffn_up(U_F1[s], s, 0)
                if s:
                    ffn_down(s - 1)
                if s < FSTEPS:
                    ffn_up(U_F3[s], s, 1)

            turn_norm(2)

            def lru_in(g, s, bank):
                use(g)
                for c in range(2):
                    for k in range(KD):
                        if g == U_X[0] and c == 0:
                            pe.wait_ge(act_lo_ready, 2 * KD + k + 1)
                        ins = product(ps[:, bank, c * SEQ:(c + 1) * SEQ],
                                      cols_of(g, k * 256 + c * P, P), tokens(k), k == 0, k == KD - 1)
                ins.then_inc(unit_used, 1)

            def lru_out(s):
                pe.wait_ge(y_lo_ready, s + 1)
                if s == 0:
                    pe.wait_ge(res_ready, 8)
                into_residual(U_O[s], lambda kk, i: tuple(t[:, kk, i * P:(i + 1) * P] for t in y_parts(s)),
                              s == 0, s == LSTEPS - 1)

            def lru_gates(s):
                use(U_GA[s])
                pe.wait_ge(xc_lo_ready, s + 1)
                for a in range(2):
                    for c in range(2):
                        ins = product(ps[:, 6 + a, c * SEQ:(c + 1) * SEQ], cols_of(U_GA[s], a * 256 + c * P, P),
                                      (lc_hi[:, c, :], lc_lo[:, c, :]), True, True)
                ins.then_inc(unit_used, 1)

            def long_rows():
                for i in range(TT):
                    for k in range(KD):
                        bias = ident[:, R_BO + k:R_BO + k + 1].to_broadcast([P, P])
                        pe.matmul(ps[:, 2 * i + k // 4, k % 4 * P:(k % 4 + 1) * P], bias, rows[:],
                                  start=False, stop=False)
                pe.wait_ge(xb_ready, 2 * LSTEPS)
                pe.wait_ge(gate_ready, 2 * LSTEPS)
                for k in range(KD):
                    r = R_FFN + KD + k
                    ins = pe.matmul(ps[:, 4 + k // 4, k % 4 * P:(k % 4 + 1) * P],
                                    ident[:, r:r + 1].to_broadcast([P, P]), rows[:], start=True, stop=True)
                ins.then_inc(gain_rows, 1)

            for kind, s in lru_steps:
                if kind == "X":
                    if s == 0:
                        pe.wait_ge(act_lo_ready, 2 * KD + 2)
                    else:
                        pe.wait_ge(xb_ready, 2 * s)
                    lru_in(U_X[s], s, 4)
                elif kind == "G":
                    if s:
                        pe.wait_ge(gate_ready, 2 * s)
                    lru_in(U_G[s], s, 5)
                elif kind == "GA":
                    if s:
                        pe.wait_ge(sig_ready, 4 * s)
                    lru_gates(s)
                    if s == LSTEPS - 1:
                        long_rows()
                else:
                    lru_out(s)

            pe.wait_ge(res_ready, R_PRE)
            for b in range(KD // 2):
                for kk in range(2):
                    for i in range(TT):
                        ins = pe.transpose(ps[:, b, kk * SEQ + i * P:kk * SEQ + (i + 1) * P],
                                           res[:, i, (2 * b + kk) * P:(2 * b + kk + 1) * P], ident[:])
                ins.then_inc(rx_turned, 1)
            pe.wait_ge(w_gained, KD)
            for i in range(TT):
                for k in range(KD):
                    pe.wait_ge(rxT_ready, k // 2 + 1)
                    ins = pe.matmul(ps[:, 6, i * E:(i + 1) * E], rxT[:, k, i * P:(i + 1) * P], w_router[:, k, :],
                                    start=k == 0, stop=k == KD - 1)
            ins.then_inc(logits_ready, 1)
            chosen = rsm[6]
            pe.wait_ge(mask_ready, 1)
            pe.matmul(ps[:, 7, 0:E], before[:], chosen[:, 0, :], start=True, stop=True)
            pe.matmul(ps[:, 7, E:2 * E], ones[:], chosen[:, 0, :], start=True, stop=False)
            pe.matmul(ps[:, 7, E:2 * E], before[:], chosen[:, 1, :], start=False, stop=True)
            pe.matmul(ps[:, 7, 2 * E:3 * E], ones[:], chosen[:, 0, :], start=True, stop=False)
            pe.matmul(ps[:, 7, 2 * E:3 * E], ones[:], chosen[:, 1, :], start=False,
                      stop=True).then_inc(ranks_ready, 1)

            def gather(base):
                pe.wait_ge(sel_ready, base + 2)
                for k in range(KD):
                    for j, src in enumerate((act_hi, act_lo)):
                        for i in range(TT):
                            ins = pe.matmul(ps[:, 2 + k // 4, k % 4 * P:(k % 4 + 1) * P],
                                            src[:, i * D + k * P:i * D + (k + 1) * P], sel[:, i, :],
                                            start=j == 0 and i == 0, stop=j == 1 and i == TT - 1)
                    if k % 4 == 3:
                        ins.then_inc(gathered, 1)

            def scatter(base, number):
                pe.wait_ge(selT_ready, number)
                for i in range(TT):
                    for b in range(2):
                        pe.wait_ge(y_lo_split, base + (b + 1))
                        pe.matmul(ps[:, 2 + 2 * i + b, :], selT[:, i * P:(i + 1) * P], y_hi[:, b * BANK:(b + 1) * BANK],
                                  start=True, stop=False)
                        pe.matmul(ps[:, 2 + 2 * i + b, :], selT[:, i * P:(i + 1) * P], y_lo[:, b * BANK:(b + 1) * BANK],
                                  start=False, stop=True).then_inc(scattered, 1)

            def one_pass(n, e, kind):
                u_base, t_base = held(pe, n * N_BODY), held(pe, n * MSTEPS)
                h_base, s_base = held(pe, n * 2), held(pe, n * 4)
                selT_count = held(pe, n + 1)

                def split(u):
                    pe.wait_ge(lo_ready, u_base + (N_PRE + u + 1))

                def up(table, t, half, bank):
                    u = table[t, half]
                    split(u)
                    for k in range(4):
                        kk = 4 * half + k
                        ins = product(ps[:, bank, :], (in_hi[:, kk * P:(kk + 1) * P], in_lo[:, kk * P:(kk + 1) * P]),
                                      cols_of(N_PRE + u, k * BANK, BANK), kk == 0, kk == KD - 1)
                    ins.then_inc(unit_used, 1)

                def turn(t):
                    pe.wait_ge(h_ready, t_base + (t + 1))
                    for c in range(4):
                        ins = pe.transpose(ps[:, 6, c * P:(c + 1) * P], e_h[t % 2][:, c * P:(c + 1) * P], ident[:])
                    ins.then_inc(h_turned, 1)

                def down(t):
                    pe.wait_ge(hT_lo_ready, t_base + (t + 1))
                    for half in range(2):
                        u = M_W2[t, half]
                        split(u)
                        for k in range(2):
                            c = 2 * half + k
                            for b in range(2):
                                ins = product(ps[:, 4 + b, :], (hT_hi[:, c * P:(c + 1) * P], hT_lo[:, c * P:(c + 1) * P]),
                                              cols_of(N_PRE + u, k * D + b * BANK, BANK),
                                              t == 0 and c == 0, t == MSTEPS - 1 and c == 3)
                        ins.then_inc(unit_used, 1)

                if kind == "extra":
                    pe.wait_ge(res_ready, s_base + (R_PRE + 4))
                    gather(h_base)
                for t in range(MSTEPS):
                    bank = 2 * (t % 2)
                    if t == 0:
                        pe.wait_ge(in_lo_ready, h_base + 1)
                    elif t == 1 and kind != "extra":
                        pe.wait_ge(res_ready, s_base + (R_PRE + 2))
                    up(M_W1, t, 0, bank)
                    if t == 0:
                        pe.wait_ge(in_lo_ready, h_base + 2)
                    up(M_W1, t, 1, bank)
                    if t == 0 and kind != "extra":
                        scatter(h_base, selT_count)
                    if t:
                        turn(t - 1)
                    if t == 1:
                        for i in range(TT):
                            pe.transpose(ps[:, 7, i * P:(i + 1) * P], sel[:, i, :].bitcast(F32), ident[:])
                        for i in range(TT):
                            ins = pe.matmul(ps[:, 7, SEQ:SEQ + 1], sel[:, i, :].bitcast(F32), gates[:, i, bass.ds(e, 1)],
                                            start=i == 0, stop=i == TT - 1)
                        ins.then_inc(selT_turned, 1)
                    up(M_W3, t, 0, bank + 1)
                    up(M_W3, t, 1, bank + 1)
                    if t == 1 and kind != "extra":
                        pe.wait_ge(res_ready, s_base + (R_PRE + 4))
                    if t:
                        down(t - 1)
                turn(MSTEPS - 1)
                if kind == "next":
                    gather(h_base + 2)
                down(MSTEPS - 1)
                if kind != "next":
                    scatter(h_base + 2, selT_count + 1)

            def first_tokens():
                pe.wait_ge(y_zeroed, 1)
                gather(0)

            experts(pe, lambda n, e, off: one_pass(n, e, "next"), first_tokens,
                    lambda n, e, off: one_pass(n, e, "last"), lambda n, e, off: one_pass(n, e, "extra"))

        @block.scalar
        def _(act):
            def hi(g):
                act.wait_ge(raw_landed[slot_of(g)], landed_at[g])
                if g >= SPLIT_SLOTS:
                    act.wait_ge(unit_used, g - SPLIT_SLOTS + 1)
                act.activation(w_hi[g % SPLIT_SLOTS][:, 0:width[g]], raw[slot_of(g)][:, 0:width[g]],
                               ACT.Copy).then_inc(hi_ready, 1)

            def norm_squares(i):
                if i == 0:
                    act.wait_ge(x_landed, 16 * TT)
                else:
                    act.wait_ge(res_ready, 4 * i - 2)
                act.activation(xn[:, 0, :], res[:, 0, :], ACT.Square, accum_out=sumsq[:, 0:1]).then_inc(sq_act, 1)

            def norm_apply(i):
                act.wait_ge(rstd_ready, i + 1)
                act.activation(xn[:, 0, :], res[:, 0, :], ACT.Copy, scale=rstd[:, 0:1]).then_inc(xn0_ready, 1)

            def norm_hi(i, gain):
                for k in range(KD):
                    act.wait_ge(xn_turned, 4 * i + k // 2 + 1)
                    act.activation(act_hi[:, k * SEQ:(k + 1) * SEQ], ps[:, 4 + k // 2, k % 2 * SEQ:(k % 2 + 1) * SEQ],
                                   ACT.Copy, scale=cols[:, gain + k:gain + k + 1]).then_inc(act_hi_ready, 1)

            norm_squares(0)
            act.wait_ge(cols_ready, 1)
            norm_hi(0, R_MIX)
            for g in range(6):
                hi(g)
            act.wait_ge(unit_used, U_WIN[-1] + 1)
            for i in range(TT):
                act.wait_ge(rstd_ready, 1)
                for c in range(2):
                    w = CAT // 2
                    act.activation(hcat[:, i, c * w:(c + 1) * w], ps[:, 2 * i + c, 0:w], ACT.Copy,
                                   scale=rstd[:, i:i + 1]).then_inc(cat_ready, 1)
            hi(6)
            act.wait_ge(cols_ready, 3)
            for c in range(LAT):
                act.wait_ge(lat_turned, min(c // 2 * 2 + 2, LAT))
                act.activation(lat_hi[:, c, :], ps[:, 4 + c // 2, c % 2 * SEQ:(c % 2 + 1) * SEQ], ACT.Copy,
                               scale=cols[:, R_QA + c:R_QA + c + 1]).then_inc(lat_hi_ready, 1)
            act.wait_ge(cat_ready, 2 * TT)
            for i in range(TT):
                cat_junk = act_junk[:, i * 1024:(i + 1) * 1024]
                act.activation(cat_junk[:, 0:Q_LORA], hcat[:, i, 0:Q_LORA], ACT.Square,
                               accum_out=sumsq[:, 2 + i:3 + i]).then_inc(cat_sq, 1)
                act.activation(cat_junk[:, Q_LORA:Q_LORA + KV_LORA], hcat[:, i, Q_LORA:Q_LORA + KV_LORA], ACT.Square,
                               accum_out=sumsq[:, 4 + i:5 + i]).then_inc(cat_sq, 1)
            act.activation(sin[:], trig[2][:], ACT.Sin).then_inc(trig_ready, 1)
            act.activation(cos[:], trig[3][:], ACT.Sin).then_inc(trig_ready, 1)
            hi(7)

            def copy_kv(j):
                for c in range(2):
                    src = ps[:, 4 * j + c, :].rearrange("p (h d) -> p h d", h=2)
                    h = 4 * j + 2 * c
                    act.activation(kn[:, 0, h:h + 2, :], src[:, :, 0:NOPE], ACT.Copy,
                                   scale=rstd[:, 4:5]).then_inc(kv0_copied, 1)
                    act.activation(vt[:, 0, h:h + 2, :], src[:, :, NOPE:], ACT.Copy,
                                   scale=rstd[:, 4:5]).then_inc(kv0_copied, 1)

            def head_squares(which, src, width, squares):
                for h in range(HEADS):
                    act.activation(squares[:, h * width:(h + 1) * width], src[:, 0, h, :], ACT.Square,
                                   accum_out=ssh[:, which, h:h + 1]).then_inc(head_sq_act, 1)

            act.wait_ge(lat_rstd, 1)

            copy_kv(0)
            hi(8)
            copy_kv(1)
            act.wait_ge(kv0_copied, 8)
            act.wait_ge(cat_sq, 4)
            head_squares(0, kn, NOPE, act_junk)
            for j in range(3):
                hi(9 + j)
                for i in range(TT):
                    q_flat = qn[:, i, :, :].rearrange("p h d -> p (h d)")
                    act.activation(q_flat[:, j * BANK:(j + 1) * BANK], ps[:, 2 * j + i, :], ACT.Copy,
                                   scale=rstd[:, 2 + i:3 + i]).then_inc(q_copied, 1)
            act.wait_ge(head_rstd, 1)
            for h in range(HEADS):
                act.activation(kn[:, 0, h, :], kn[:, 0, h, :], ACT.Copy, scale=rsh[:, 0, h:h + 1]).then_inc(kn0_scaled, 1)
            act.wait_ge(q_copied, 6)
            head_squares(1, qn, QK_HEAD, q_junk)
            act.wait_ge(const_ready, 2)
            for b in range(0, 12, 2):
                bank = (6 + b) % 8
                act.wait_ge(kq_turned, b + 1)
                src = ps[:, bank, :].rearrange("p (a t) -> p a t", a=2)
                if b < 4:
                    act.activation(qT[:, 2 * b:2 * b + 2, :], src, ACT.Copy,
                                   scale=cols[:, R_QN:R_QN + 1]).then_inc(kqT_act, 1)
                elif b < 8:
                    act.activation(kT[:, 2 * (b - 4):2 * (b - 4) + 2, :], src, ACT.Copy,
                                   scale=cols[:, R_KN:R_KN + 1]).then_inc(kqT_act, 1)
                elif b < 10:
                    act.activation(krT[:, 2 * (b - 8):2 * (b - 8) + 2, :], src, ACT.Copy).then_inc(kqT_act, 1)
                else:
                    h = 4 * (b - 10)
                    act.activation(qrT[0:ROPE, h:h + 4:2, :], src[0:ROPE], ACT.Copy).then_inc(kqT_act, 1)
                    act.activation(qrT[ROPE:P, h + 1:h + 4:2, :], src[ROPE:P], ACT.Copy).then_inc(kqT_act, 1)

            def exps(h):
                act.wait_ge(smax_ready, h + 1)
                if h >= 4:
                    act.wait_ge(probs_turned, h - 3)
                for i in range(TT):
                    at = slice(i * P, i * P + (i + 1) * P)
                    act.activation(pr[h % 4][:, at], ps[:, h % 4, at], ACT.Exp, bias=smax[:, h, i:i + 1],
                                   scale=rsh[:, 1, i * HEADS + h:i * HEADS + h + 1],
                                   accum_out=ssum[:, h, i:i + 1]).then_inc(exp_ready, 1)

            def probs_T(h):
                act.wait_ge(probs_turned, h + 1)
                if h >= 2:
                    act.wait_ge(pv_ready, h - 1)
                act.activation(prT[h % 2][:], ps[:, 4 + h % 2, 0:3 * P], ACT.Copy).then_inc(probsT_ready, 1)

            def head_hi(h):
                act.wait_ge(pv_ready, h + 1)
                act.activation(act_hi[:, h * SEQ:(h + 1) * SEQ], ps[:, 6 + h % 2, 0:SEQ],
                               ACT.Copy).then_inc(o_hi_ready, 1)

            for h in range(HEADS + 3):
                if h < HEADS:
                    exps(h)
                if 2 <= h < HEADS + 2:
                    probs_T(h - 2)
                if h >= 3:
                    head_hi(h - 3)
            for g in range(12, 15):
                hi(g)

            norm_squares(1)
            norm_apply(1)
            hi(15)
            norm_hi(1, R_FFN)

            def f_gate(s):
                b = 4 + 2 * (s % 2)
                act.wait_ge(unit_used, U_F1[s] + 1)
                act.activation(f_h[s % 2][:], ps[:, b, :], ACT.Silu).then_inc(f_silu, 1)

            def f_split(s):
                act.wait_ge(f_h_ready, s + 1)
                act.activation(f_hi[:], f_h[s % 2][:], ACT.Copy).then_inc(f_hi_ready, 1)

            hi(N_ATT + 3)
            f_gate(0)
            hi(N_ATT + 4)
            f_split(0)
            act.wait_ge(lam_ready, 1)
            act.activation(lam[1][:], lam[0][:], ACT.Exp).then_inc(lam_exp, 1)
            for s in range(1, FSTEPS):
                hi(U_F1[s] + 3)
                f_gate(s)
                hi(U_F1[s] + 4)
                f_split(s)
                hi(U_F1[s] + 5)

            norm_squares(2)
            norm_apply(2)
            norm_hi(2, R_MIX + KD)

            def x_work(s):
                act.wait_ge(unit_used, U_X[s] + 1)
                if s:
                    act.wait_ge(conv_ready, 2 * s)
                for c in range(2):
                    b = R_BIN + KD + 2 * s + c
                    act.activation(xpad[:, c, 3:3 + SEQ], ps[:, 4, c * SEQ:(c + 1) * SEQ], ACT.Identity,
                                   bias=cols[:, b:b + 1]).then_inc(xb_ready, 1)
                if s == 0:
                    conv_hi(0)

            def conv_hi(s):
                act.wait_ge(conv_ready, 2 * (s + 1))
                act.activation(lc_hi[:], xc[:], ACT.Copy).then_inc(xc_hi_ready, 1)

            def g_work(s):
                if s:
                    act.wait_ge(y_ready, s)
                act.wait_ge(unit_used, U_G[s] + 1)
                for c in range(2):
                    b = R_BIN + 2 * s + c
                    act.activation(gate[:, c, :], ps[:, 5, c * SEQ:(c + 1) * SEQ], ACT.Gelu_apprx_tanh,
                                   bias=cols[:, b:b + 1]).then_inc(gate_ready, 1)

            def a_work(s):
                act.wait_ge(unit_used, U_GA[s] + 1)
                if s:
                    act.wait_ge(y_hi_ready, s)
                    act.wait_ge(y_lo_ready, s)
                for a, dst in enumerate((ra, iu)):
                    for c in range(2):
                        b = (R_BA, R_BI)[a] + 2 * s + c
                        act.activation(dst[:, c, :], ps[:, 6 + a, c * SEQ:(c + 1) * SEQ], ACT.Sigmoid,
                                       bias=cols[:, b:b + 1]).then_inc(sig_ready, 1)
                act.wait_ge(sig_ready, 4 * s + 2)
                for c in range(2):
                    h = 2 * s + c
                    act.activation(tm[:, c, :], ra[:, c, :], ACT.Tanh, scale=decay[:, 0, h:h + 1]).then_inc(at_ready, 1)
                for c in range(2):
                    h = 2 * s + c
                    act.activation(ra[:, c, :], ra[:, c, :], ACT.Exp, scale=decay[:, 1, h:h + 1]).then_inc(at_ready, 1)
                if s + 1 < LSTEPS:
                    hi(U_GA[s] + SPLIT_SLOTS)
                    conv_hi(s + 1)
                act.wait_ge(v_ready, s + 1)
                act.activation(tm[:], tm[:], ACT.Sqrt).then_inc(mult_ready, 1)
                act.wait_ge(y_ready, s + 1)
                if s == LSTEPS - 2:
                    act.wait_ge(unit_used, U_G[LSTEPS - 1] + 1)
                act.activation(y_parts(s)[0], iu[:], ACT.Copy).then_inc(y_hi_ready, 1)
                if s + 1 == LSTEPS:
                    hi(U_GA[s] + SPLIT_SLOTS)

            lru_order(hi, x_work, g_work, a_work)

            norm_squares(3)
            act.wait_ge(sq_act, 4)
            act.wait_ge(sq_dve, 4)
            for b in range(KD // 2):
                act.wait_ge(rx_turned, b + 1)
                act.activation(rxT[:, 2 * b:2 * b + 2, :], ps[:, b, :].rearrange("p (k t) -> p k t", k=2),
                               ACT.Copy).then_inc(rxT_ready, 1)
            for i in range(TT):
                act.wait_ge(rx_ready, 2 * (i + 1))
                act.activation(act_hi[:, i * D:(i + 1) * D], rx[:, i, :], ACT.Copy).then_inc(tok_hi_ready, 1)
            act.wait_ge(top_ready, 1)
            act.activation(rsm[3][:, :, 0:1], rsm[2][:, :, 0:1], ACT.Exp).then_inc(top_exp, 1)
            hi(N_PRE + 2)
            act.wait_ge(routed, 1)

            def take_in(base):
                for b in range(2):
                    act.wait_ge(gathered, base + (b + 1))
                    act.activation(in_hi[:, b * BANK:(b + 1) * BANK], ps[:, 2 + b, :], ACT.Copy).then_inc(in_hi_ready, 1)

            def hi_of(u_base, l_base, u):
                slot = slot_of(N_PRE + u)
                landed = slot_count[slot] + 16 * (u // RAW_SLOTS + 1)
                act.wait_ge(raw_landed[slot], l_base + landed)
                act.wait_ge(unit_used, u_base + (N_PRE + u - SPLIT_SLOTS + 1))
                act.activation(w_hi[(N_PRE + u) % SPLIT_SLOTS][:], raw[slot][:], ACT.Copy).then_inc(hi_ready, 1)

            def one_pass(n, kind):
                u_base, t_base = held(act, n * N_BODY), held(act, n * MSTEPS)
                h_base, l_base = held(act, n * 2), held(act, n * (16 * OCC))

                def silu(t):
                    act.wait_ge(unit_used, u_base + (N_PRE + M_W1[t, 1] + 1))
                    if t == 0 and kind != "extra":
                        act.wait_ge(scattered, n * 4 + 4)
                    act.activation(e_h[t % 2][:], ps[:, 2 * (t % 2), :], ACT.Silu).then_inc(silu_ready, 1)

                def turned(t):
                    act.wait_ge(h_turned, t_base + (t + 1))
                    act.activation(hT_hi[:], ps[:, 6, :], ACT.Copy).then_inc(hT_hi_ready, 1)

                if kind == "extra":
                    hi_of(u_base, l_base, 0)
                    take_in(h_base)
                    hi_of(u_base, l_base, 1)
                    hi_of(u_base, l_base, 2)
                for u in range(3, N_BODY):
                    hi_of(u_base, l_base, u)
                    for t in range(MSTEPS):
                        if u == M_W1[t, 1] + 3:
                            silu(t)
                            if t:
                                turned(t - 1)
                            if t == 1:
                                act.wait_ge(selT_turned, n + 1)
                                act.activation(selT[:], ps[:, 7, 0:SEQ], ACT.Copy).then_inc(selT_ready, 1)
                                act.activation(slot_gate[:], ps[:, 7, SEQ:SEQ + 1], ACT.Copy).then_inc(gate_col_ready, 1)
                turned(MSTEPS - 1)
                if kind == "next":
                    take_in(h_base + 2)
                    for u in range(3):
                        hi_of(u_base, l_base, N_BODY + u)
                act.wait_ge(unit_used, u_base + (N_PRE + N_BODY))
                act.wait_ge(gate_col_ready, n + 1)
                for b in range(2):
                    act.activation(y_hi[:, b * BANK:(b + 1) * BANK], ps[:, 4 + b, :], ACT.Copy,
                                   scale=slot_gate[:, 0:1]).then_inc(out_hi_ready, 1)

            def first_tokens():
                act.activation(selT[:], slot_ids[:], ACT.Copy, scale=0.0).then_inc(selT_ready, 1)
                take_in(0)

            experts(act, lambda n, e, off: one_pass(n, "next"), first_tokens,
                    lambda n, e, off: one_pass(n, "last"), lambda n, e, off: one_pass(n, "extra"))

        @block.vector
        def _(dve):
            own = Chain(dve, dve_own)

            def lo(g):
                dve.wait_ge(hi_ready, g + 1)
                s, w = g % SPLIT_SLOTS, width[g]
                dve.tensor_tensor(w_lo[s][:, 0:w], raw[slot_of(g)][:, 0:w], w_hi[s][:, 0:w].bitcast(F32),
                                  ALU.subtract).then_inc(lo_ready, 1)

            def norm_scale(i):
                if i == 0:
                    dve.wait_ge(x_landed, 16 * TT)
                else:
                    dve.wait_ge(res_ready, 4 * i)
                dve.tensor_tensor_reduce(xn[:, 1, :], res[:, 1, :], res[:, 1, :], 1.0, 0.0, ALU.mult, ALU.add,
                                         sumsq[:, 1:2]).then_inc(sq_dve, 1)

            def norm_apply(i):
                dve.wait_ge(rstd_ready, i + 1)
                dve.tensor_scalar(xn[:, 1, :], res[:, 1, :], rstd[:, 1:2], None, ALU.mult).then_inc(xn_ready, 1)

            def norm_lo(i, gain):
                for k in range(KD):
                    dve.wait_ge(act_hi_ready, KD * i + k // 2 * 2 + 2)
                    at = slice(k * SEQ, (k + 1) * SEQ)
                    dve.scalar_tensor_tensor(out=act_lo[:, at], in0=ps[:, 4 + k // 2, k % 2 * SEQ:(k % 2 + 1) * SEQ],
                                             scalar=cols[:, gain + k:gain + k + 1], in1=act_hi[:, at].bitcast(F32),
                                             op0=ALU.mult, op1=ALU.subtract).then_inc(act_lo_ready, 1)

            norm_scale(0)
            dve.wait_ge(rows_turned, 1)
            dve.tensor_copy(cols[:, 0:R_FFN], ps[:, 0, 0:R_FFN]).then_inc(cols_ready, 1)
            norm_lo(0, R_MIX)
            for g in range(3):
                lo(g)
            dve.wait_ge(pos_landed, 32)
            posf, turns, red, halfr = trig
            own.link(dve.tensor_copy(ssr[:], pos_i[:]))
            for i in range(TT):
                own.step(dve.tensor_scalar(posf[:, i, :], freq[:], ssr[:, i:i + 1], None, ALU.mult))
            own.settle()
            own.link(dve.tensor_scalar(turns[:], posf[:], 1.0 / (2 * np.pi), ROUND_MAGIC, ALU.mult, ALU.add))
            own.link(dve.tensor_scalar(turns[:], turns[:], -ROUND_MAGIC, None, ALU.add))
            own.link(dve.scalar_tensor_tensor(out=red[:], in0=turns[:], scalar=-TWO_PI_A, in1=posf[:],
                                              op0=ALU.mult, op1=ALU.add))
            own.link(dve.scalar_tensor_tensor(out=red[:], in0=turns[:], scalar=-TWO_PI_B, in1=red[:],
                                              op0=ALU.mult, op1=ALU.add))
            own.link(dve.scalar_tensor_tensor(out=red[:], in0=turns[:], scalar=-TWO_PI_C, in1=red[:],
                                              op0=ALU.mult, op1=ALU.add))
            own.link(dve.tensor_scalar(red[:], red[:], -PI_FLOOR, PI_FLOOR, ALU.max, ALU.min))
            own.link(dve.tensor_scalar(halfr[:], red[:], 0.5, None, ALU.mult))
            for g in range(3, 6):
                lo(g)
            dve.wait_ge(rows_turned, 2)
            own.step(dve.tensor_copy(g_rope[:], ps[:, 7, P:2 * P]))
            dve.tensor_copy(cols[:, R_FFN:P], ps[:, 7, R_FFN:P]).then_inc(cols_ready, 2)
            for c in range(LAT):
                dve.wait_ge(lat_hi_ready, min(c // 2 * 2 + 2, LAT))
                dve.scalar_tensor_tensor(out=lat_lo[:, c, :], in0=ps[:, 4 + c // 2, c % 2 * SEQ:(c % 2 + 1) * SEQ],
                                         scalar=cols[:, R_QA + c:R_QA + c + 1], in1=lat_hi[:, c, :].bitcast(F32),
                                         op0=ALU.mult, op1=ALU.subtract).then_inc(lat_lo_ready, 1)
            lo(6)

            dve.wait_ge(cat_ready, 2 * TT)
            for i in range(TT):
                dve.tensor_tensor_reduce(junk[:, 1536 + i * ROPE:1536 + (i + 1) * ROPE], hcat[:, i, CAT - ROPE:],
                                         hcat[:, i, CAT - ROPE:], 1.0, 0.0, ALU.mult, ALU.add,
                                         ssr[:, i:i + 1]).then_inc(head_sq, 1)
            dve.wait_ge(head_sq, TT)
            dve.wait_ge(trig_ready, 2)
            own.link(dve.tensor_tensor(cos[:], cos[:], cos[:], ALU.mult))
            own.step(dve.tensor_scalar(cos[:], cos[:], -2.0, 1.0, ALU.mult, ALU.add))

            def rope(x1, x2, o1, o2, shape, done=None):
                t = [r[:][tuple(slice(0, n) for n in shape)] for r in rope_t]
                c = cos[:].unsqueeze(2).to_broadcast(shape)
                s = sin[:].unsqueeze(2).to_broadcast(shape)
                for dst, a, b in ((t[0], x1, c), (t[1], x2, s), (t[2], x1, s), (t[3], x2, c)):
                    own.step(dve.tensor_tensor(dst, a, b, ALU.mult))
                own.settle()
                for ins in (dve.tensor_tensor(o1, t[0], t[1], ALU.subtract),
                            dve.tensor_tensor(o2, t[2], t[3], ALU.add)):
                    ins.then_inc(done, 1) if done else own.step(ins)
                own.settle()

            kshape = [P, TT, 1, HALF]
            krope = hcat[:, :, CAT - ROPE:].unsqueeze(2)
            k_gain = g_rope[:, ROPE:].unsqueeze(1).unsqueeze(1).to_broadcast([P, TT, 1, ROPE])
            own.link(dve.tensor_tensor(krope, krope, k_gain, ALU.mult))
            rope(krope[:, :, :, 0:HALF], krope[:, :, :, HALF:], krope[:, :, :, 0:HALF], krope[:, :, :, HALF:], kshape)
            lo(7)

            def copy_kv(j):
                dve.wait_ge(unit_used, U_KV[j] + 1)
                for c in range(2):
                    src = ps[:, 4 * j + 2 + c, :].rearrange("p (h d) -> p h d", h=2)
                    h = 4 * j + 2 * c
                    dve.tensor_scalar(kn[:, 1, h:h + 2, :], src[:, :, 0:NOPE], rstd[:, 5:6], None,
                                      ALU.mult).then_inc(kv1_copied, 1)
                    dve.tensor_scalar(vt[:, 1, h:h + 2, :], src[:, :, NOPE:], rstd[:, 5:6], None,
                                      ALU.mult).then_inc(kv1_copied, 1)

            dve.wait_ge(lat_rstd, 1)
            copy_kv(0)
            lo(8)
            copy_kv(1)
            lo(9)
            dve.wait_ge(kv1_copied, 8)
            for h in range(HEADS):
                dve.tensor_tensor_reduce(junk[:, h * NOPE:(h + 1) * NOPE], kn[:, 1, h, :], kn[:, 1, h, :], 1.0,
                                         0.0, ALU.mult, ALU.add,
                                         ssh[:, 0, HEADS + h:HEADS + h + 1]).then_inc(head_sq, 1)
            lo(10)
            lo(11)
            dve.wait_ge(head_rstd, 1)
            k_scale = rsh[:, 0, :].rearrange("p (i h) -> p i h", h=HEADS).unsqueeze(3)
            dve.tensor_tensor(kn[:, 1], kn[:, 1], k_scale[:, 1].to_broadcast([P, HEADS, NOPE]),
                              ALU.mult).then_inc(kq_normed, 1)
            for i in range(TT):
                dve.tensor_tensor(kr[:, i], krope[:, i].to_broadcast([P, HEADS, ROPE]),
                                  k_scale[:, i].to_broadcast([P, HEADS, ROPE]), ALU.mult).then_inc(kq_normed, 1)
            dve.wait_ge(q_copied, 6)
            for i in range(TT):
                own.step(dve.tensor_tensor(qr[:, i], qn[:, i, :, NOPE:],
                                           g_rope[:, 0:ROPE].unsqueeze(1).to_broadcast([P, HEADS, ROPE]), ALU.mult))
            own.settle()
            dve.wait_ge(head_sq, TT + HEADS)
            rope(qr[:, :, :, 0:HALF], qr[:, :, :, HALF:], qr[:, :, :, 0:HALF], qr[:, :, :, HALF:],
                 [P, TT, HEADS, HALF], kq_normed)
            q_scale = rsh[:, 1, :].rearrange("p (i h) -> p i h", h=HEADS)
            for b in range(1, 12, 2):
                bank = (6 + b) % 8
                if b == 9:
                    dve.wait_ge(kq_normed, 5)
                    for h in range(HEADS):
                        dve.tensor_tensor_reduce(junk[:, h * QK_HEAD:(h + 1) * QK_HEAD], qn[:, 1, h, :], qn[:, 1, h, :], 1.0,
                                                 0.0, ALU.mult, ALU.add,
                                                 ssh[:, 1, HEADS + h:HEADS + h + 1]).then_inc(head_sq, 1)
                dve.wait_ge(kq_turned, b + 1)
                src = ps[:, bank, :].rearrange("p (a t) -> p a t", a=2)
                if b < 4:
                    dve.tensor_scalar(qT[:, 2 * b:2 * b + 2, :], src, cols[:, R_QN:R_QN + 1], None,
                                      ALU.mult).then_inc(kqT_dve, 1)
                elif b < 8:
                    dve.tensor_scalar(kT[:, 2 * (b - 4):2 * (b - 4) + 2, :], src, cols[:, R_KN:R_KN + 1], None,
                                      ALU.mult).then_inc(kqT_dve, 1)
                elif b < 10:
                    dve.tensor_copy(krT[:, 2 * (b - 8):2 * (b - 8) + 2, :], src).then_inc(kqT_dve, 1)
                else:
                    h = 4 * (b - 10)
                    dve.tensor_copy(qrT[0:ROPE, h:h + 4:2, :], src[0:ROPE]).then_inc(kqT_dve, 1)
                    dve.tensor_copy(qrT[ROPE:P, h + 1:h + 4:2, :], src[ROPE:P]).then_inc(kqT_dve, 1)

            def score_max(h):
                dve.wait_ge(scores_ready, h + 1)
                for i in range(TT):
                    own.step(dve.tensor_reduce(smax[:, h, i:i + 1], ps[:, h % 4, i * P:i * P + (i + 1) * P], AX.X, ALU.max))
                own.settle()
                dve.scalar_tensor_tensor(out=smax[:, h, :], in0=smax[:, h, :], scalar=-1.0, in1=q_scale[:, :, h],
                                         op0=ALU.mult, op1=ALU.mult).then_inc(smax_ready, 1)

            def normalise(h):
                dve.wait_ge(exp_ready, 2 * h + 2)
                own.link(dve.reciprocal(sinv[:, h, :], ssum[:, h, :]))
                for i in range(TT):
                    at = slice(i * P, i * P + (i + 1) * P)
                    dve.tensor_scalar(pr[h % 4][:, at], pr[h % 4][:, at], sinv[:, h, i:i + 1], None,
                                      ALU.mult).then_inc(probs_ready, 1)

            def head_lo(h):
                dve.wait_ge(o_hi_ready, h + 1)
                at = slice(h * SEQ, (h + 1) * SEQ)
                dve.tensor_tensor(act_lo[:, at], ps[:, 6 + h % 2, 0:SEQ], act_hi[:, at].bitcast(F32),
                                  ALU.subtract).then_inc(o_lo_ready, 1)

            dve.wait_ge(head_rstd, 2)
            for h in range(HEADS + 3):
                if h < HEADS:
                    score_max(h)
                if 1 <= h <= HEADS:
                    normalise(h - 1)
                if h >= 3:
                    head_lo(h - 3)

            def add_residual(last_unit, n):
                for i in range(TT):
                    for c in range(2):
                        if (i, c) == (TT - 1, 1):
                            dve.wait_ge(unit_used, last_unit + 1)
                        else:
                            dve.wait_ge(sum_ready, 3 * n + 2 * i + c + 1)
                        at = slice(c * BANK, (c + 1) * BANK)
                        dve.tensor_tensor(res[:, i, at], res[:, i, at], ps[:, 2 * i + c, :], ALU.add).then_inc(res_ready, 1)

            for g in range(12, 14):
                lo(g)
            add_residual(U_WO[-1], 0)

            norm_scale(1)
            norm_apply(1)
            norm_lo(1, R_FFN)
            lo(14)
            lo(15)

            def f_mult(s):
                b = 4 + 2 * (s % 2)
                h = f_h[s % 2][:]
                dve.wait_ge(unit_used, U_F3[s] + 1)
                dve.wait_ge(f_silu, s + 1)
                dve.tensor_tensor(h, h, ps[:, b + 1, :], ALU.mult).then_inc(f_h_ready, 1)
                dve.wait_ge(f_hi_ready, s + 1)
                dve.tensor_tensor(f_lo[:], f_h[s % 2][:], f_hi[:].bitcast(F32), ALU.subtract).then_inc(f_lo_ready, 1)

            lo(N_ATT + 3)
            f_mult(0)
            lo(N_ATT + 4)
            dve.wait_ge(small_landed, 32)
            for k in range(KD):
                r = R_FFN + KD + k
                dve.tensor_scalar(w_router[:, k, :], w_router[:, k, :], cols[:, r:r + 1], None,
                                  ALU.mult).then_inc(w_gained, 1)
            absl, z, d, w, w2, acc = lam
            lam_cols = cols[:, R_LAM:R_LAM + LRU_HEADS]
            own.link(dve.tensor_scalar(d[:], lam_cols, -1.0, None, ALU.mult))
            dve.tensor_tensor(absl[:], lam_cols, d[:], ALU.min).then_inc(lam_ready, 1)
            dve.wait_ge(lam_exp, 1)
            own.link(dve.tensor_scalar(d[:], z[:], 2.0, None, ALU.add))
            own.link(dve.reciprocal(d[:], d[:]))
            own.link(dve.tensor_tensor(w[:], z[:], d[:], ALU.mult))
            own.link(dve.tensor_tensor(w2[:], w[:], w[:], ALU.mult))
            own.link(dve.memset(acc[:], 2.0 / 19))
            for k in range(17, 0, -2):
                own.link(dve.tensor_tensor(acc[:], acc[:], w2[:], ALU.mult))
                own.link(dve.tensor_scalar(acc[:], acc[:], 2.0 / k, None, ALU.add))
            own.link(dve.tensor_tensor(acc[:], acc[:], w[:], ALU.mult))
            own.link(dve.tensor_scalar(d[:], cols[:, R_LAM:R_LAM + LRU_HEADS], 0.0, None, ALU.min))
            own.link(dve.tensor_tensor(d[:], d[:], acc[:], ALU.subtract))
            own.step(dve.tensor_scalar(decay[:, 0, :], d[:], -8.0, None, ALU.mult))
            own.link(dve.tensor_scalar(decay[:, 1, :], d[:], 8.0, None, ALU.mult))
            for s in range(1, FSTEPS):
                lo(U_F1[s] + 3)
                lo(U_F1[s] + 4)
                f_mult(s)
                if s < FSTEPS - 1:
                    lo(U_F1[s] + 5)
            add_residual(U_F2[FSTEPS - 1], 1)

            norm_scale(2)
            norm_apply(2)
            norm_lo(2, R_MIX + KD)
            lo(U_G[0])
            own.link(dve.memset(xpad[:, :, 0:3], 0.0))

            def x_work(s):
                if s == 0:
                    conv(0)
                    conv_lo(0)

            def conv(s):
                dve.wait_ge(xb_ready, 2 * (s + 1))
                for c in range(2):
                    h = 2 * s + c

                    def tap(j):
                        return cols[:, R_CW + j * KD + h:R_CW + j * KD + h + 1]

                    own.step(dve.tensor_scalar(xc[:, c, :], xpad[:, c, 0:SEQ], tap(0), cols[:, R_CB + h:R_CB + h + 1],
                                               ALU.mult, ALU.add))
                own.settle()
                for j in range(1, 4):
                    for c in range(2):
                        h = 2 * s + c
                        w_j = cols[:, R_CW + j * KD + h:R_CW + j * KD + h + 1]
                        ins = dve.scalar_tensor_tensor(out=xc[:, c, :], in0=xpad[:, c, j:j + SEQ], scalar=w_j,
                                                       in1=xc[:, c, :], op0=ALU.mult, op1=ALU.add)
                        ins.then_inc(conv_ready, 1) if j == 3 else own.step(ins)
                    own.settle()

            def conv_lo(s):
                dve.wait_ge(xc_hi_ready, s + 1)
                dve.tensor_tensor(lc_lo[:], xc[:], lc_hi[:].bitcast(F32), ALU.subtract).then_inc(xc_lo_ready, 1)

            def a_work(s):
                dve.wait_ge(sig_ready, 4 * (s + 1))
                own.link(dve.tensor_tensor(iu[:], iu[:], xc[:], ALU.mult))
                if s + 1 < LSTEPS:
                    conv(s + 1)
                dve.wait_ge(at_ready, 4 * s + 4)
                own.link(dve.tensor_tensor(a_squared[:], ra[:], ra[:], ALU.mult))
                dve.scalar_tensor_tensor(out=tm[:], in0=a_squared[:], scalar=1.0, in1=tm[:], op0=ALU.add,
                                         op1=ALU.mult).then_inc(v_ready, 1)
                if s + 1 < LSTEPS:
                    dve.wait_ge(v_ready, s + 1)
                    conv_lo(s + 1)
                    lo(U_GA[s] + SPLIT_SLOTS)
                dve.wait_ge(mult_ready, s + 1)
                own.link(dve.tensor_tensor(iu[:], iu[:], tm[:], ALU.mult))
                for c in range(2):
                    own.step(dve.tensor_tensor_scan(iu[:, c, :], ra[:, c, :], iu[:, c, :], 0.0, ALU.mult, ALU.add))
                own.settle()
                dve.wait_ge(gate_ready, 2 * (s + 1))
                dve.tensor_tensor(iu[:], iu[:], gate[:], ALU.mult).then_inc(y_ready, 1)
                dve.wait_ge(y_hi_ready, s + 1)
                y_hi_part, y_lo_part = y_parts(s)
                dve.tensor_tensor(y_lo_part, iu[:], y_hi_part.bitcast(F32), ALU.subtract).then_inc(y_lo_ready, 1)
                if s + 1 == LSTEPS:
                    lo(U_GA[s] + SPLIT_SLOTS)

            lru_order(lo, x_work, None, a_work)
            add_residual(U_O[LSTEPS - 1], 2)

            norm_scale(3)
            dve.wait_ge(rstd_ready, 4)
            dve.wait_ge(gain_rows, 1)
            for i in range(TT):
                for c in range(2):
                    at = slice(c * BANK, (c + 1) * BANK)
                    dve.scalar_tensor_tensor(out=rx[:, i, at], in0=res[:, i, at], scalar=rstd[:, i:i + 1],
                                             in1=ps[:, 4 + c, :], op0=ALU.mult, op1=ALU.mult).then_inc(rx_ready, 1)
            for i in range(TT):
                dve.wait_ge(tok_hi_ready, i + 1)
                at = slice(i * D, (i + 1) * D)
                dve.tensor_tensor(act_lo[:, at], rx[:, i, :], act_hi[:, at].bitcast(F32),
                                  ALU.subtract).then_inc(tok_lo_ready, 1)
            logits, top, diff, ediff, first, second, chosen, weight, idx_f, tmp = rsm
            shape = [P, TT, E]
            dve.wait_ge(logits_ready, 1)
            for i in range(TT):
                own.step(dve.scalar_tensor_tensor(out=logits[:, i, :], in0=ps[:, 6, i * E:(i + 1) * E],
                                                  scalar=rstd[:, i:i + 1], in1=b_router[:], op0=ALU.mult, op1=ALU.add))
            own.settle()
            for i in range(TT):
                own.step(dve.max(top[:, i, :], logits[:, i, :]))
            own.settle()
            for i in range(TT):
                own.step(dve.max_index(ridx[:, i, :], top[:, i, :], logits[:, i, :]))
            dve.tensor_tensor(diff[:, :, 0:1], top[:, :, 1:2], top[:, :, 0:1], ALU.subtract).then_inc(top_ready, 1)
            own.settle()
            own.link(dve.tensor_copy(idx_f[:], ridx[:]))
            ids = expert_ids[:].unsqueeze(1).to_broadcast(shape)
            own.step(dve.tensor_tensor(first[:], ids, idx_f[:, :, 0:1].to_broadcast(shape), ALU.is_equal))
            own.link(dve.tensor_tensor(second[:], ids, idx_f[:, :, 1:2].to_broadcast(shape), ALU.is_equal))
            dve.tensor_tensor(chosen[:], first[:], second[:], ALU.add).then_inc(mask_ready, 1)
            dve.wait_ge(top_exp, 1)
            own.link(dve.tensor_scalar(weight[:, :, 0:1], ediff[:, :, 0:1], 1.0, None, ALU.add))
            own.link(dve.reciprocal(weight[:, :, 0:1], weight[:, :, 0:1]))
            own.link(dve.tensor_tensor(weight[:, :, 1:2], weight[:, :, 0:1], ediff[:, :, 0:1], ALU.mult))
            own.step(dve.tensor_tensor(first[:], first[:], weight[:, :, 0:1].to_broadcast(shape), ALU.mult))
            own.link(dve.tensor_tensor(second[:], second[:], weight[:, :, 1:2].to_broadcast(shape), ALU.mult))
            own.step(dve.tensor_tensor(gates[:], first[:], second[:], ALU.add))
            dve.wait_ge(ranks_ready, 1)
            own.link(dve.tensor_scalar(tmp[:], ps[:, 7, 0:TT * E].rearrange("p (i e) -> p i e", e=E), MISS, None, ALU.add))
            own.link(dve.tensor_tensor(tmp[:], tmp[:], chosen[:], ALU.mult))
            own.step(dve.tensor_scalar(rank[:], tmp[:], -MISS, None, ALU.add))
            own.settle()
            dve.wait_ge(tok_lo_ready, 2)
            dve.tensor_copy(counts[:], ps[:, 7, 2 * E:3 * E]).then_inc(routed, 1)

            def select(e, off):
                for i in range(TT):
                    dve.tensor_scalar(sel[:, i, :], slot_ids[:, off:off + P], rank[:, i, bass.ds(e, 1)], None,
                                      ALU.is_equal).then_inc(sel_ready, 1)

            def take_in(base):
                for b in range(2):
                    dve.wait_ge(in_hi_ready, base + (b + 1))
                    at = slice(b * BANK, (b + 1) * BANK)
                    dve.tensor_tensor(in_lo[:, at], ps[:, 2 + b, :], in_hi[:, at].bitcast(F32),
                                      ALU.subtract).then_inc(in_lo_ready, 1)

            def lo_of(u_base, u):
                dve.wait_ge(hi_ready, u_base + (N_PRE + u + 1))
                s = (N_PRE + u) % SPLIT_SLOTS
                dve.tensor_tensor(w_lo[s][:], raw[slot_of(N_PRE + u)][:], w_hi[s][:].bitcast(F32),
                                  ALU.subtract).then_inc(lo_ready, 1)

            def add_scattered(base):
                for i in range(TT):
                    for b in range(2):
                        dve.wait_ge(scattered, base + (2 * i + b + 1))
                        at = slice(b * BANK, (b + 1) * BANK)
                        dve.tensor_tensor(res[:, i, at], res[:, i, at], ps[:, 2 + 2 * i + b, :],
                                          ALU.add).then_inc(res_ready, 1)

            def one_pass(n, e, off, kind):
                u_base, t_base = held(dve, n * N_BODY), held(dve, n * MSTEPS)
                h_base, s_base = held(dve, n * 2), held(dve, n * 4)

                def mult(t):
                    dve.wait_ge(unit_used, u_base + (N_PRE + M_W3[t, 1] + 1))
                    dve.wait_ge(silu_ready, t_base + (t + 1))
                    dve.tensor_tensor(e_h[t % 2][:], e_h[t % 2][:], ps[:, 2 * (t % 2) + 1, :],
                                      ALU.mult).then_inc(h_ready, 1)

                def turned(t):
                    dve.wait_ge(hT_hi_ready, t_base + (t + 1))
                    dve.tensor_tensor(hT_lo[:], ps[:, 6, :], hT_hi[:].bitcast(F32), ALU.subtract).then_inc(hT_lo_ready, 1)

                if kind == "extra":
                    select(e, off)
                    lo_of(u_base, 0)
                    take_in(h_base)
                    lo_of(u_base, 1)
                    lo_of(u_base, 2)
                for u in range(3, N_BODY):
                    lo_of(u_base, u)
                    if u == M_W1[0, 1] + 3 and kind != "extra":
                        dve.wait_ge(res_ready, s_base + R_PRE)
                        add_scattered(s_base)
                    if u == M_W1[2, 1] + 3 and kind == "next":
                        dve.wait_ge(selT_turned, n + 1)
                        select(e + 1, 0)
                    for t in range(MSTEPS):
                        if t and u == M_W1[t, 1] + 3:
                            turned(t - 1)
                        if u == M_W3[t, 1] + 2:
                            mult(t)
                turned(MSTEPS - 1)
                if kind == "next":
                    take_in(h_base + 2)
                    for u in range(3):
                        lo_of(u_base, N_BODY + u)
                for b in range(2):
                    dve.wait_ge(out_hi_ready, h_base + (b + 1))
                    at = slice(b * BANK, (b + 1) * BANK)
                    dve.scalar_tensor_tensor(out=y_lo[:, at], in0=ps[:, 4 + b, :], scalar=slot_gate[:, 0:1],
                                             in1=y_hi[:, at].bitcast(F32), op0=ALU.mult,
                                             op1=ALU.subtract).then_inc(y_lo_split, 1)
                if kind != "next":
                    dve.wait_ge(res_ready, s_base + (R_PRE + 4))
                    add_scattered(s_base + 4)

            def first_tokens():
                dve.wait_ge(routed, 1)
                select(0, 0)
                lo(N_PRE + 2)
                take_in(0)
                dve.memset(y_lo[:].bitcast(F32), 0.0).then_inc(y_lo_split, 2)

            experts(dve, lambda n, e, off: one_pass(n, e, off, "next"), first_tokens,
                    lambda n, e, off: one_pass(n, e, off, "last"), lambda n, e, off: one_pass(n, e, off, "extra"))


_INS = ["x", "positions", "norm_mix", "norm_ffn", "mla_w_in", "mla_g_qa", "mla_w_qb", "mla_g_kva", "mla_w_kvb",
        "mla_g_qn", "mla_g_kn", "mla_w_o", "lru_w_in", "lru_b_in", "lru_conv_w", "lru_conv_b", "lru_w_gate_a",
        "lru_b_gate_a", "lru_w_gate_i", "lru_b_gate_i", "lru_lambda", "lru_w_out", "lru_b_out", "ffn_w1",
        "ffn_w3", "ffn_w2", "moe_w_router", "moe_b_router", "moe_w1", "moe_w3", "moe_w2"]


def kernel(**inputs):
    import numpy as _np
    import concourse.bacc as _bacc
    from concourse import mybir as _mybir
    from concourse.bass_utils import run_bass_kernel_spmd as _run

    nc = _bacc.Bacc("TRN2", target_bir_lowering=False, num_devices=1)
    arrays = {f"in_{name}_dram": _np.ascontiguousarray(inputs[name]) for name in _INS}
    rope = inputs["mla_g_qn"].shape[1] - 128
    exponents = _np.arange(0, rope, 2, dtype=_np.float32) / _np.float32(rope)
    arrays["rope_freq_dram"] = (_np.float32(1.0) / _np.power(_np.float32(ROPE_BASE), exponents)).astype(_np.float32)
    args = [nc.dram_tensor(name, a.shape, _mybir.dt.from_np(a.dtype), kind="ExternalInput").ap()
            for name, a in arrays.items()]
    shape = inputs["x"].shape
    args.append(nc.dram_tensor("out_dram", shape, _mybir.dt.float32, kind="ExternalOutput").ap())
    encoder_trunk(nc, *args)
    return _run(nc, [arrays], core_ids=[0]).results[0]["out_dram"]
```
